# Optimizing a Trainium2 kernel written in Bass

```python
import jax, jax.numpy as jnp
from jax import lax
import numpy as np

'''One inference step of a 4-layer hybrid decoder trunk, with shared weights for a prompt group and a sample group.

Layers 0 and 2 (even): RMSNorm -> one combined input projection whose columns are split into
  mixer A (short gated convolution, 512 channels = 8 groups of 64): gates B, C and value xv, y_A = B * conv3(C * xv)
  mixer B (dilated sliding-window attention, 8 heads x 64, NoPE): q, k, v; every head evaluates the three
    (window, dilation) branches (128,1), (512,4), (2048,16) over strided gathered keys and the branch outputs
    are merged with weights proportional to their softmax denominators
  -> concat [y_A | y_B] -> one output projection -> residual add.
Layers 1 and 3 (odd): RMSNorm -> multi-scale causal pooling (4 channel groups of 256 with trailing windows
  2, 4, 8, 16; mean minus token) -> per-group linear map -> per-channel scale -> residual add.
Every layer: RMSNorm -> PEER product-key expert retrieval (8 heads, 128x128 single-neuron experts, top-16) -> residual add.
Final RMSNorm.

Inputs:
  x_prompt (BATCH, SEQ, D_MODEL), positions 0..SEQ-1
  x_sample (DEC_BATCH, DEC_SEQ, D_MODEL), positions PAST_LEN..PAST_LEN+DEC_SEQ-1
  state_conv  (N_EVEN, DEC_BATCH, CONV_W-1, D_CONV)                 last 2 rows of C*xv
  state_win_k (N_EVEN, DEC_BATCH, min(WINDOW_MAX, PAST_LEN), N_HEADS_B, HEAD_DIM_B)  last key rows
  state_win_v (N_EVEN, DEC_BATCH, min(WINDOW_MAX, PAST_LEN), N_HEADS_B, HEAD_DIM_B)  last value rows
  state_pool  (N_ODD, DEC_BATCH, POOL_STATE, D_MODEL)                last 15 normalised rows
  followed by the weights.
Returns (y_prompt, y_sample, conv_prompt, conv_sample, win_k_prompt, win_k_sample,
         win_v_prompt, win_v_sample, pool_prompt, pool_sample):
  y_prompt (BATCH, SEQ, D_MODEL), y_sample (DEC_BATCH, DEC_SEQ, D_MODEL)
  conv_prompt (N_EVEN, BATCH, 2, D_CONV), conv_sample (N_EVEN, DEC_BATCH, 2, D_CONV)
  win_k_prompt / win_v_prompt (N_EVEN, BATCH, min(WINDOW_MAX, SEQ), N_HEADS_B, HEAD_DIM_B)
  win_k_sample / win_v_sample (N_EVEN, DEC_BATCH, min(WINDOW_MAX, PAST_LEN), N_HEADS_B, HEAD_DIM_B)
  pool_prompt (N_ODD, BATCH, 15, D_MODEL), pool_sample (N_ODD, DEC_BATCH, 15, D_MODEL)
'''

D_MODEL = 1024
BATCH = 1
SEQ = 512
DEPTH = 2
DEC_BATCH = 8
DEC_SEQ = 1
PAST_LEN = 1024
PAGE_SIZE = 128

N_EVEN = (DEPTH + 1) // 2
N_ODD = DEPTH // 2
D_CONV = D_MODEL // 2
CONV_W = 3
N_HEADS_B = 8
HEAD_DIM_B = (D_MODEL // 2) // N_HEADS_B
D_ATT = N_HEADS_B * HEAD_DIM_B
DILATED_PAIRS = ((128, 1), (512, 4), (2048, 16))
WINDOW_MAX = max(w for w, _ in DILATED_PAIRS)
ATT_BLOCK = 128
NEG_INF = -1e30
POOL_WINDOWS = (2, 4, 8, 16)
POOL_GROUP = D_MODEL // len(POOL_WINDOWS)
POOL_STATE = max(POOL_WINDOWS) - 1
PEER_HEADS = 8
PEER_QDIM = 256
PEER_HALF = PEER_QDIM // 2
N_KEYS = 128
N_EXPERTS = N_KEYS * N_KEYS
PEER_TOPK = 16
PEER_CHUNK = 256
NORM_EPS = 1e-6

kernel_name = 'hybrid_conv_dilated_pool_peer_step'

def rms_norm(x, g):
    x32 = x.astype(jnp.float32)
    r = lax.rsqrt(jnp.mean(x32 * x32, axis=-1, keepdims=True) + NORM_EPS)
    return (x32 * r).astype(x.dtype) * g

def split_projection(h, w_in):
    p = h @ w_in
    cuts = [D_CONV, 2 * D_CONV, 3 * D_CONV, 3 * D_CONV + D_ATT, 3 * D_CONV + 2 * D_ATT]
    return jnp.split(p, cuts, axis=-1)

def gated_short_conv(gate_b, u_hist, conv_w):
    T = gate_b.shape[1]
    y = conv_w[0] * u_hist[:, 0:T]
    for i in range(1, CONV_W):
        y = y + conv_w[i] * u_hist[:, i:i + T]
    return gate_b * y

def to_heads(t):
    return t.reshape(t.shape[0], t.shape[1], N_HEADS_B, HEAD_DIM_B)

def dilated_branch_prompt(q, k, v, window, dil):
    b, S, H, hd = q.shape
    n_back = window // dil
    L = S // dil
    nb = -(-L // ATT_BLOCK)
    pad_end = nb * ATT_BLOCK - L

    def residues(t):
        return t.reshape(b, L, dil, H, hd).transpose(0, 2, 1, 3, 4).reshape(b * dil, L, H, hd)

    qb = jnp.pad(residues(q), ((0, 0), (0, pad_end), (0, 0), (0, 0))).reshape(b * dil, nb, ATT_BLOCK, H, hd)

    def band(t):
        tb = jnp.pad(residues(t), ((0, 0), (ATT_BLOCK, pad_end), (0, 0), (0, 0)))
        tb = tb.reshape(b * dil, nb + 1, ATT_BLOCK, H, hd)
        return jnp.concatenate([tb[:, :-1], tb[:, 1:]], axis=2)

    kb, vb = band(k), band(v)
    s = jnp.einsum('bnqhd,bnkhd->bnhqk', qb, kb)
    qi = jnp.arange(ATT_BLOCK)[:, None]
    ki = jnp.arange(2 * ATT_BLOCK)[None, :]
    dist = qi + ATT_BLOCK - ki
    key_pos = (jnp.arange(nb) * ATT_BLOCK - ATT_BLOCK)[:, None, None] + ki[None]
    mask = ((dist >= 0) & (dist <= n_back))[None] & (key_pos >= 0)
    s = jnp.where(mask[None, :, None], s, NEG_INF)
    m = jnp.max(s, axis=-1, keepdims=True)
    p = jnp.exp(s - m)
    den = jnp.sum(p, axis=-1)
    o = jnp.einsum('bnhqk,bnkhd->bnqhd', p, vb) / den.transpose(0, 1, 3, 2)[..., None]
    lse = (m[..., 0] + jnp.log(den)).transpose(0, 1, 3, 2)
    o = o.reshape(b * dil, nb * ATT_BLOCK, H, hd)[:, :L]
    lse = lse.reshape(b * dil, nb * ATT_BLOCK, H)[:, :L]
    o = o.reshape(b, dil, L, H, hd).transpose(0, 2, 1, 3, 4).reshape(b, S, H, hd)
    lse = lse.reshape(b, dil, L, H).transpose(0, 2, 1, 3).reshape(b, S, H)
    return o, lse

def dilated_branch_sample(q, k_all, v_all, window, dil, wb):
    T = q.shape[1]
    n_back = window // dil
    idx = wb + jnp.arange(T)[:, None] - jnp.arange(n_back + 1)[None, :] * dil
    valid = idx >= 0
    idx = jnp.maximum(idx, 0)
    kg = k_all[:, idx]
    vg = v_all[:, idx]
    s = jnp.einsum('bthd,btjhd->bhtj', q, kg)
    s = jnp.where(valid[None, None], s, NEG_INF)
    m = jnp.max(s, axis=-1, keepdims=True)
    p = jnp.exp(s - m)
    den = jnp.sum(p, axis=-1)
    o = jnp.einsum('bhtj,btjhd->bthd', p, vg) / den.transpose(0, 2, 1)[..., None]
    lse = (m[..., 0] + jnp.log(den)).transpose(0, 2, 1)
    return o, lse

def combine_branches(branches):
    o = jnp.stack([br[0] for br in branches])
    lse = jnp.stack([br[1] for br in branches])
    wts = jax.nn.softmax(lse, axis=0)
    return jnp.sum(wts[..., None] * o, axis=0)

def even_mixer_prompt(h, w_in, conv_w, w_out):
    b, S, _ = h.shape
    gate_b, gate_c, xv, q, k, v = split_projection(h, w_in)
    u_hist = jnp.pad(gate_c * xv, ((0, 0), (CONV_W - 1, 0), (0, 0)))
    y_a = gated_short_conv(gate_b, u_hist, conv_w)
    q, k, v = to_heads(q), to_heads(k), to_heads(v)
    qf = q.astype(jnp.float32) * HEAD_DIM_B ** -0.5
    kf, vf = k.astype(jnp.float32), v.astype(jnp.float32)
    y_b = combine_branches([dilated_branch_prompt(qf, kf, vf, w, d) for w, d in DILATED_PAIRS])
    y_b = y_b.reshape(b, S, D_ATT).astype(h.dtype)
    out = jnp.concatenate([y_a, y_b], axis=-1) @ w_out
    wb = min(WINDOW_MAX, S)
    return out, u_hist[:, -(CONV_W - 1):], k[:, S - wb:], v[:, S - wb:]

def even_mixer_sample(h, conv_state, k_state, v_state, w_in, conv_w, w_out):
    b, T, _ = h.shape
    gate_b, gate_c, xv, q, k, v = split_projection(h, w_in)
    u_hist = jnp.concatenate([conv_state.astype(h.dtype), gate_c * xv], axis=1)
    y_a = gated_short_conv(gate_b, u_hist, conv_w)
    q, k, v = to_heads(q), to_heads(k), to_heads(v)
    wb = k_state.shape[1]
    k_all = jnp.concatenate([k_state.astype(h.dtype), k], axis=1)
    v_all = jnp.concatenate([v_state.astype(h.dtype), v], axis=1)
    qf = q.astype(jnp.float32) * HEAD_DIM_B ** -0.5
    kf, vf = k_all.astype(jnp.float32), v_all.astype(jnp.float32)
    y_b = combine_branches([dilated_branch_sample(qf, kf, vf, w, d, wb) for w, d in DILATED_PAIRS])
    y_b = y_b.reshape(b, T, D_ATT).astype(h.dtype)
    out = jnp.concatenate([y_a, y_b], axis=-1) @ w_out
    return out, u_hist[:, -(CONV_W - 1):], k_all[:, -wb:], v_all[:, -wb:]

def pool_mix(u, pool_w, pool_b, pool_scale, n_out):
    b, L, _ = u.shape
    u32 = u.astype(jnp.float32)
    csum = jnp.concatenate([jnp.zeros_like(u32[:, :1]), jnp.cumsum(u32, axis=1)], axis=1)
    rows = jnp.arange(1, L + 1, dtype=jnp.float32)
    groups = []
    for g, w in enumerate(POOL_WINDOWS):
        c = csum[:, :, g * POOL_GROUP:(g + 1) * POOL_GROUP]
        lagged = jnp.pad(c[:, :L + 1 - w], ((0, 0), (w - 1, 0), (0, 0)))
        mean = (c[:, 1:] - lagged) / jnp.minimum(rows, w)[None, :, None]
        groups.append(mean - u32[:, :, g * POOL_GROUP:(g + 1) * POOL_GROUP])
    y = jnp.stack(groups, axis=2)[:, L - n_out:].astype(u.dtype)
    y = jnp.einsum('btgc,gcd->btgd', y, pool_w) + pool_b
    return y.reshape(b, n_out, D_MODEL) * pool_scale

def peer_ffn(h, wq, subkeys, u_tab, v_tab):
    b, T, D = h.shape
    n = b * T
    chunk = min(PEER_CHUNK, n)
    n_chunks = -(-n // chunk)
    hc = jnp.pad(h.reshape(n, D), ((0, n_chunks * chunk - n), (0, 0))).reshape(n_chunks, chunk, D)
    sk = subkeys.astype(jnp.float32)

    def retrieve(hb):
        q = (hb @ wq).astype(jnp.float32).reshape(chunk, PEER_HEADS, 2, PEER_HALF)
        s = jnp.einsum('nhcd,hckd->nhck', q, sk)
        sv, si = lax.top_k(s, PEER_TOPK)
        cand = (sv[:, :, 0, :, None] + sv[:, :, 1, None, :]).reshape(chunk, PEER_HEADS, PEER_TOPK * PEER_TOPK)
        cs, ci = lax.top_k(cand, PEER_TOPK)
        i1 = jnp.take_along_axis(si[:, :, 0], ci // PEER_TOPK, axis=-1)
        i2 = jnp.take_along_axis(si[:, :, 1], ci % PEER_TOPK, axis=-1)
        expert = i1 * N_KEYS + i2
        g = jax.nn.softmax(cs, axis=-1)
        act = jax.nn.gelu(jnp.einsum('nd,nhkd->nhk', hb, u_tab[expert]).astype(jnp.float32), approximate=False)
        return jnp.einsum('nhk,nhkd->nd', (g * act).astype(hb.dtype), v_tab[expert])

    out = lax.map(retrieve, hc)
    return out.reshape(n_chunks * chunk, D)[:n].reshape(b, T, D)

def setup_inputs(seed: int = 0) -> dict:
    key = jax.random.key(seed)
    ks = jax.random.split(key, 20)
    f32 = jnp.float32
    wb = min(WINDOW_MAX, PAST_LEN)

    def nrm(k, shape, scale):
        return jax.random.normal(k, shape, f32) * scale

    return {
        'x_prompt': nrm(ks[0], (BATCH, SEQ, D_MODEL), 1.0),
        'x_sample': nrm(ks[1], (DEC_BATCH, DEC_SEQ, D_MODEL), 1.0),
        'state_conv': nrm(ks[2], (N_EVEN, DEC_BATCH, CONV_W - 1, D_CONV), 1.0),
        'state_win_k': nrm(ks[3], (N_EVEN, DEC_BATCH, wb, N_HEADS_B, HEAD_DIM_B), 1.0),
        'state_win_v': nrm(ks[4], (N_EVEN, DEC_BATCH, wb, N_HEADS_B, HEAD_DIM_B), 1.0),
        'state_pool': nrm(ks[5], (N_ODD, DEC_BATCH, POOL_STATE, D_MODEL), 1.0),
        'norm_mix': 1.0 + nrm(ks[6], (DEPTH, D_MODEL), 0.1),
        'w_in_ab': nrm(ks[7], (N_EVEN, D_MODEL, 3 * D_CONV + 3 * D_ATT), D_MODEL ** -0.5),
        'conv_w': nrm(ks[8], (N_EVEN, CONV_W, D_CONV), 0.5),
        'w_out_ab': nrm(ks[9], (N_EVEN, D_CONV + D_ATT, D_MODEL), (D_CONV + D_ATT) ** -0.5),
        'pool_w': nrm(ks[10], (N_ODD, len(POOL_WINDOWS), POOL_GROUP, POOL_GROUP), POOL_GROUP ** -0.5),
        'pool_b': nrm(ks[11], (N_ODD, len(POOL_WINDOWS), POOL_GROUP), 0.01),
        'pool_scale': 1.0 + nrm(ks[12], (N_ODD, D_MODEL), 0.1),
        'norm_ffn': 1.0 + nrm(ks[13], (DEPTH, D_MODEL), 0.1),
        'peer_wq': nrm(ks[14], (DEPTH, D_MODEL, PEER_HEADS * PEER_QDIM), D_MODEL ** -0.5),
        'peer_subkeys': nrm(ks[15], (DEPTH, PEER_HEADS, 2, N_KEYS, PEER_HALF), PEER_HALF ** -0.5),
        'peer_u': nrm(ks[16], (DEPTH, N_EXPERTS, D_MODEL), D_MODEL ** -0.5),
        'peer_v': nrm(ks[17], (DEPTH, N_EXPERTS, D_MODEL), 0.2),
        'norm_final': 1.0 + nrm(ks[18], (D_MODEL,), 0.1),
    }

def reference(x_prompt, x_sample, state_conv, state_win_k, state_win_v, state_pool,
              norm_mix, w_in_ab, conv_w, w_out_ab, pool_w, pool_b, pool_scale,
              norm_ffn, peer_wq, peer_subkeys, peer_u, peer_v, norm_final):
    xp, xs = x_prompt, x_sample
    conv_p, conv_s, wk_p, wk_s, wv_p, wv_s, pool_p, pool_s = [], [], [], [], [], [], [], []
    for l in range(DEPTH):
        hp = rms_norm(xp, norm_mix[l])
        hs = rms_norm(xs, norm_mix[l])
        if l % 2 == 0:
            e = l // 2
            op, cp, kp, vp = even_mixer_prompt(hp, w_in_ab[e], conv_w[e], w_out_ab[e])
            osm, cs, ksm, vsm = even_mixer_sample(hs, state_conv[e], state_win_k[e], state_win_v[e],
                                                  w_in_ab[e], conv_w[e], w_out_ab[e])
            conv_p.append(cp); conv_s.append(cs)
            wk_p.append(kp); wk_s.append(ksm)
            wv_p.append(vp); wv_s.append(vsm)
        else:
            o = l // 2
            op = pool_mix(hp, pool_w[o], pool_b[o], pool_scale[o], hp.shape[1])
            pool_p.append(hp[:, -POOL_STATE:])
            hcat = jnp.concatenate([state_pool[o].astype(hs.dtype), hs], axis=1)
            osm = pool_mix(hcat, pool_w[o], pool_b[o], pool_scale[o], hs.shape[1])
            pool_s.append(hcat[:, -POOL_STATE:])
        xp = xp + op
        xs = xs + osm
        xp = xp + peer_ffn(rms_norm(xp, norm_ffn[l]), peer_wq[l], peer_subkeys[l], peer_u[l], peer_v[l])
        xs = xs + peer_ffn(rms_norm(xs, norm_ffn[l]), peer_wq[l], peer_subkeys[l], peer_u[l], peer_v[l])
    y_prompt = rms_norm(xp, norm_final)
    y_sample = rms_norm(xs, norm_final)
    return (y_prompt, y_sample, jnp.stack(conv_p), jnp.stack(conv_s), jnp.stack(wk_p), jnp.stack(wk_s),
            jnp.stack(wv_p), jnp.stack(wv_s), jnp.stack(pool_p), jnp.stack(pool_s))


_drawn_inputs = setup_inputs


def setup_inputs(seed=0):
    import zlib

    import numpy as np

    out = dict(_drawn_inputs(seed))
    spreads = {}
    factors = {'pool_b': 6.141}
    for name, (base, spread) in spreads.items():
        noise = np.random.default_rng([zlib.crc32(name.encode()), seed]).standard_normal(out[name].shape)
        drawn = base * np.exp(spread * noise) if base else spread * noise
        out[name] = __import__('jax').numpy.asarray(drawn.astype(out[name].dtype))
    for name, factor in factors.items():
        out[name] = (out[name] * factor).astype(out[name].dtype)
    return out
```

```python
import concourse.bass as bass
from concourse import mybir
from concourse.alu_op_type import AluOpType as ALU
from contextlib import ExitStack

f32 = mybir.dt.float32
u32 = mybir.dt.uint32
i32 = mybir.dt.int32
ACT = mybir.ActivationFunctionType
AX = mybir.AxisListType

P = 128
D = 1024
KD = D // P
SEQ = 512
T = SEQ // P
B = 8
L = 2
NH = 8
HD = 64
DA = NH * HD
CA = DA // P
PAST = 1024
PH = 8
HC = 2 * PH
NK = 128
NE = NK * NK
TOP = 16
EPS = 1e-6
NEG = -1e30
LOWEST = -3.0e38
POOL_W = (2, 4, 8, 16)
NG = len(POOL_W)
GW = D // NG
PS = max(POOL_W) - 1
WC = 256
HT_N = SEQ + B
NB = 6
SLOTS = 8
DIAGS = 4
SETS = 4
SAMPLE_ROWS = 65
LOC = (P, P, SAMPLE_ROWS)


def psum_jobs():
    jobs = []

    def rows_transposed(key):
        for t in range(T):
            for half in range(2):
                jobs.append((key, t, half))
        jobs.append((key, "s"))

    def queries(l):
        for hc in range(HC):
            jobs.extend([("q", l, hc), ("qs", l, hc), ("sc", l, hc), ("scs", l, hc)])

    for j in range(4):
        jobs.append(("skT", 0, j))
    rows_transposed("hT_mix")
    jobs.extend([("conv_state",), ("conv_w",)])
    for ch in (2, 3, 4, 5, 0, 1, 6, 7, 8, 9):
        for half in range(2):
            jobs.extend([("p", ch, half), ("ps", ch, half)])
    for ch in (10, 11):
        for t in range(T + 1):
            jobs.append(("v", ch, t))
    jobs.extend([("kn", t) for t in range(T)] + [("kns",), ("qns",), ("utail",), ("us",)])
    n = T * NH
    jobs.append(("s", 0))
    for m in range(n):
        if m + 1 < n:
            jobs.append(("s", m + 1))
        jobs.append(("pT", m))
        if m >= 1 and (m - 1) % NH == NH - 1:
            jobs.append(("yT", (m - 1) // NH))
    jobs.append(("yT", T - 1))
    for b in range(B):
        jobs.append(("qrep", b))
    jobs.extend([("ssT",), ("spT",)])
    for b in range(B):
        jobs.append(("so", b))
    for t in range(T + 1):
        for half in range(2):
            jobs.append(("wo", t, half))
    rows_transposed("hT_ffn0")
    queries(0)
    for j in range(4):
        jobs.append(("skT", 1, j))
    for t in range(T):
        jobs.extend([("pp", t, 0), ("pp", t, 1), ("pl", t, 0), ("pl", t, 1)])
    jobs.extend([("pps",), ("pl", T, 0), ("pl", T, 1)])
    rows_transposed("hT_ffn1")
    queries(1)
    return {name: (i % NB, i // NB) for i, name in enumerate(jobs)}


def build(nc, x_prompt, x_sample, state_conv, state_win_k, state_win_v, state_pool, norm_mix, w_in_ab,
          conv_w, w_out_ab, pool_w, pool_b, pool_scale, norm_ffn, peer_wq, peer_subkeys, peer_u, peer_v,
          norm_final, y_prompt, y_sample, conv_prompt, conv_sample, win_k_prompt, win_k_sample,
          win_v_prompt, win_v_sample, pool_prompt, pool_sample):
    JOBS = psum_jobs()
    ctx = ExitStack()
    with ctx:
        def sb(name, shape, dt=f32):
            return ctx.enter_context(nc.sbuf_tensor(name, shape, dt))

        def sem(name):
            return ctx.enter_context(nc.semaphore(name))

        X = sb("X", [P, T + 1, D])
        H = sb("H", [P, (T + 1) * D])
        Hv = H[:, :].rearrange("p (s d) -> p s d", d=D)
        HT = sb("HT", [P, KD, HT_N])
        SC = sb("SC", [P, T * HC * NK + 2 * NK])
        RING = sb("RING", [P, 2 * SLOTS * D])
        SKT = sb("SKT", [P, HC, NK])
        G = sb("G", [P, D])
        hcur = sb("hcur", [P, D])
        hrep = sb("hrep", [P, D])
        ident = sb("ident", [P, P])
        zeros = sb("zeros", [P, P])
        COUNT = sb("COUNT", [P, T, P])
        MASKED = sb("MASKED", [P, T, P])
        POOL_CUR = sb("POOL_CUR", [P, NG, P])
        POOL_PREV = sb("POOL_PREV", [P, NG, P])
        POOL_FIRST = sb("POOL_FIRST", [P, NG, P])
        POOL_STATE_M = sb("POOL_STATE_M", [P, NG, B])
        POOL_NEW_M = sb("POOL_NEW_M", [P, NG, B])
        tplus1 = sb("tplus1", [P, P])
        diag = sb("diag", [P, DIAGS, P])
        Y = sb("Y", [P, 2, DA])
        v_s = sb("v_s", [P, DA])
        sel64 = sb("sel64", [P, B])
        ones = sb("ones", [P, 1])
        convw = sb("convw", [P, 3, CA])
        conv_st = sb("conv_st", [P, CA, B, 2])
        c_s = sb("c_s", [P, CA, B])
        u_s = sb("u_s", [P, CA, B])
        qT_s = sb("qT_s", [P, CA, B])
        kT_s = sb("kT_s", [P, CA, B])
        q_s2 = sb("q_s2", [P, 2, B])
        pT_s = sb("pT_s", [P, KD, B])
        ss = sb("ss", [P, T + 1])
        rstd = sb("rstd", [P, T + 1])
        negm = sb("negm", [P, 2])
        den = sb("den", [P, 2, NH])
        rden = sb("rden", [P, 2, NH])
        iota16 = sb("iota16", [P, TOP])
        W = sb("W", [P, 4 * 2 * NK])
        sc = W[:, 0:2 * NK].rearrange("p (c k) -> p c k", c=2)
        scw = W[:, 2 * NK:4 * NK].rearrange("p (c k) -> p c k", c=2)
        cand = W[:, 4 * NK:6 * NK]
        candw = W[:, 6 * NK:8 * NK]
        onehot = sb("onehot", [P, 2, TOP, TOP])
        sv = sb("sv", [P, 2, TOP])
        si = sb("si", [P, 2, TOP], u32)
        sif = sb("sif", [P, 2, TOP])
        ci = sb("ci", [P, TOP], u32)
        cij = sb("cij", [P, 2, TOP], u32)
        cijf = sb("cijf", [P, 2, TOP])
        picked = sb("picked", [P, 2, TOP])
        cs = sb("cs", [P, SETS, TOP])
        ncs = sb("ncs", [P, SETS])
        idx = sb("idx", [P, SETS, TOP], u32)
        ex = sb("ex", [P, SETS, TOP])
        exsum = sb("exsum", [P, SETS])
        rsum = sb("rsum", [P, 1])
        dots = sb("dots", [P, SETS, TOP])
        act_h = sb("act_h", [P, SETS, TOP])
        gate = sb("gate", [P, SETS, TOP])

        u_rows = RING[:, 0:SLOTS * D].rearrange("p (s d) -> p s d", d=D)
        v_rows = RING[:, SLOTS * D:].rearrange("p (s d) -> p s d", d=D)
        CH = KD * WC

        def wslot(base, n):
            return RING[:, base + n * CH:base + (n + 1) * CH].rearrange("p (k n) -> p k n", n=WC)

        w_in_slot = [wslot(0, n) for n in range(3)]
        wq_slot = [wslot(4 * CH, n) for n in range(3)]
        cT = RING[:, 3 * CH:4 * CH].rearrange("p (c n) -> p c n", c=CA)
        qT = RING[:, 4 * CH:5 * CH].rearrange("p (c n) -> p c n", c=CA)
        kT = RING[:, 5 * CH:6 * CH].rearrange("p (c n) -> p c n", c=CA)
        vn = RING[:, 6 * CH:7 * CH].rearrange("p (t n) -> p t n", t=T)
        sk_nat = RING[:, 7 * CH:8 * CH].rearrange("p (h d) -> p h d", h=HC)
        w_out = RING[:, 0:4 * CH].rearrange("p (k n) -> p k n", n=D)
        qp = RING[:, 3 * CH + D:4 * CH].rearrange("p (a n) -> p a n", a=2)
        sc_s = RING[:, 0:CH]
        poolw = RING[:, 0:CH].rearrange("p (g k n) -> p g k n", g=NG, k=2)
        pscale = RING[:, CH:CH + D]
        pbias = RING[:, CH + D:2 * CH]
        pT = RING[:, 2 * CH:3 * CH].rearrange("p (a c n) -> p a c n", a=2, c=KD)
        pstate = RING[:, 3 * CH:3 * CH + D]
        yT = SC[:, 0:KD * HT_N].rearrange("p (k n) -> p k n", k=KD)
        UW = SEQ + 2
        uT = SC[:, KD * HT_N:KD * HT_N + CA * UW].rearrange("p (c n) -> p c n", c=CA)
        o = KD * HT_N + CA * UW
        S = SC[:, o:o + 2 * SEQ].rearrange("p (a n) -> p a n", a=2)
        PT = SC[:, o + 2 * SEQ:o + 4 * SEQ].rearrange("p (a n) -> p a n", a=2)
        SCt = SC[:, 0:T * HC * NK].rearrange("p (t h k) -> p t h k", t=T, h=HC)
        sc64 = SC[:, T * HC * NK:T * HC * NK + 2 * NK]
        kstage = hcur[:, :].rearrange("p (a n) -> p a n", a=2)
        q_s = hrep[:, 0:DA]
        k_s = hrep[:, DA:2 * DA]
        KV = 3 * DA
        kv = H[:, 0:2 * KV].rearrange("p (a t n) -> p a t n", a=2, t=3)
        prod = H[:, 2 * KV:3 * KV]
        masked = (H[:, 3 * KV:3 * KV + DA], prod[:, 0:DA])
        sel = W[:, :].rearrange("p (b n) -> p b n", b=B)
        utail = onehot[:, :, :, :].rearrange("p a b c -> p (a b c)")
        unew = diag[:, :, :].rearrange("p a b -> p (a b)")
        dist = COUNT[:, :, :].bitcast(i32)
        S_all = Y[:, 0, 0:3 * B * NH].rearrange("p (t b h) -> p t b h", t=3, b=B)
        conv_rows = Y[0:3 * CA, 1, 0:P]
        onehot_row = cand[:, 0:P]
        POOL_STEPS = 8 + 4 * NG
        SP_ = Y[:, 1, 0:2 * P + SAMPLE_ROWS]
        SPT = S[:, 0, 0:3 * B * NH].rearrange("p (t n) -> p t n", t=3)

        PSUM = ctx.enter_context(nc.psum_tensor("PSUM", [P, 8, 512], f32))

        bank_full = [sem(f"bank_full{b}") for b in range(NB)]
        bank_emptied = [sem(f"bank_emptied{b}") for b in range(NB)]
        x_loaded = sem("x_loaded")
        g_loaded = sem("g_loaded")
        small_loaded = sem("small_loaded")
        sk_loaded = sem("sk_loaded")
        w_loaded = [sem(f"w_loaded{n}") for n in range(3)]
        wq_loaded = [sem(f"wq_loaded{n}") for n in range(3)]
        wout_loaded = sem("wout_loaded")
        kv_loaded = [sem(f"kv_loaded{n}") for n in range(2)]
        pool_loaded = sem("pool_loaded")
        sample_moved = sem("sample_moved")
        stored = sem("stored")
        pool_stored = sem("pool_stored")
        kstage_stored = [sem(f"kstage_stored{n}") for n in range(2)]
        cache_copied = [sem(f"cache_copied{n}") for n in range(2)]
        pool_consts = sem("pool_consts")
        consts = sem("consts")
        dve_chain = sem("dve_chain")
        dve_loop = sem("dve_loop")
        squares_ready = sem("squares_ready")
        root_ready = sem("root_ready")
        rows_normed = sem("rows_normed")
        kv_cleared = sem("kv_cleared")
        max_ready = sem("max_ready")
        exp_ready = sem("exp_ready")
        probs_ready = sem("probs_ready")
        y_done = sem("y_done")
        y_normed = sem("y_normed")
        k_scored = sem("k_scored")
        sy_done = sem("sy_done")
        sy_moved = sem("sy_moved")
        sprobs_ready = sem("sprobs_ready")
        smax_ready = sem("smax_ready")
        sexp_ready = sem("sexp_ready")
        u_landed = [sem(f"u_landed{s}") for s in range(SLOTS)]
        v_landed = [sem(f"v_landed{s}") for s in range(SLOTS)]
        u_freed = sem("u_freed")
        v_freed = sem("v_freed")
        idx_ready = sem("idx_ready")
        cs_ready = sem("cs_ready")
        gates_exp = sem("gates_exp")
        gelu_done = sem("gelu_done")
        gate_ready = sem("gate_ready")
        diag_ready = sem("diag_ready")
        acc_done = sem("acc_done")
        acc_added = sem("acc_added")
        passed = sem("passed")

        def bank(name):
            return PSUM[:, JOBS[name][0], :]

        def wait_full(eng, name):
            b, use = JOBS[name]
            eng.wait_ge(bank_full[b], use + 1)

        def emptied(ins, name):
            ins.then_inc(bank_emptied[JOBS[name][0]], 1)

        def wait_emptied(eng, name):
            b, use = JOBS[name]
            eng.wait_ge(bank_emptied[b], use + 1)

        def task(l, i, h):
            return l * (T * PH + 1) + i * PH + h

        def sample_task(l):
            return l * (T * PH + 1) + T * PH

        def unit(l, n):
            return l * (T + 2) + n

        block = ctx.enter_context(nc.Block())

        @block.sync
        def _(sp):
            stores = [0]

            def store(out, src):
                stores[0] += 16
                sp.dma_start(out, src).then_inc(stored, 16)

            for t in range(T):
                sp.dma_start(X[:, t + 1, :], x_prompt[0, t * P:(t + 1) * P, :]).then_inc(x_loaded, 16)
            sp.wait_ge(consts, 1)
            sp.dma_start(X[0:B, 0, :], x_sample.rearrange("b s d -> (b s) d")).then_inc(x_loaded, 16)
            sp.dma_start(G[:], norm_mix[0:1, :].to_broadcast([P, D])).then_inc(g_loaded, 16)
            sp.dma_start(sk_nat, peer_subkeys[0].rearrange("h c k d -> k (h c) d")).then_inc(sk_loaded, 16)
            sp.dma_start(conv_rows, conv_w[0].rearrange("i (c p) -> (i c) p", p=P)).then_inc(small_loaded, 16)
            sp.dma_start(Y[0:2 * B, 0, :], state_conv[0].rearrange("b j n -> (b j) n")).then_inc(small_loaded, 16)
            w_in = w_in_ab[0].rearrange("(k p) n -> p k n", p=P)
            order = (2, 3, 4, 5, 0, 1, 6, 7, 8, 9, 10, 11)
            for n, ch in enumerate(order):
                if n >= 3:
                    last = order[n - 3]
                    wait_full(sp, ("ps", last, 1))
                sp.dma_start(w_in_slot[n % 3], w_in[:, :, ch * WC:(ch + 1) * WC]).then_inc(w_loaded[n % 3], 16)
            sp.dma_start(conv_sample[0, :, 0, :], state_conv[0, :, 1, :]).then_inc(stored, 16)
            stores[0] += 16
            store(pool_sample[0, :, 0:PS - 1, :], state_pool[0, :, 1:PS, :])
            for t in range(T):
                wait_emptied(sp, ("kn", t))
                sp.dma_start(win_k_prompt[0, t * P:(t + 1) * P, :], kstage[:, t % 2, :]).then_inc(kstage_stored[t % 2], 16)
            for t in range(T):
                wait_emptied(sp, ("v", 10, t))
                wait_emptied(sp, ("v", 11, t))
                store(win_v_prompt[0, t * P:(t + 1) * P, :], vn[:, t, :])
            wait_emptied(sp, ("v", 11, T))
            wait_emptied(sp, ("kns",))
            store(win_k_sample[0, :, PAST - 1, :], k_s[0:B, :])
            store(win_v_sample[0, :, PAST - 1, :], v_s[0:B, :])
            wait_emptied(sp, ("utail",))
            wait_emptied(sp, ("us",))
            store(conv_prompt[0, 0, :, :], utail[0:2, :])
            store(conv_sample[0, :, 1, :], unew[0:B, :])
            sp.wait_ge(kv_cleared, 1)
            for n in range(2 * B):
                b, a = n % B, n % 2
                cache, own = (state_win_k, k_s) if n < B else (state_win_v, v_s)
                if n >= 2:
                    if n - 2 < B:
                        sp.wait_ge(k_scored, n - 1)
                    else:
                        wait_full(sp, ("so", n - 2 - B))
                sp.dma_start(kv[:, a, 0, :], cache[0, b, PAST - P:PAST, :]).then_inc(kv_loaded[a], 16)
                sp.dma_start(kv[:, a, 1, :], cache[0, b, PAST - 4 * P:PAST, :].rearrange("(r s) n -> r s n", s=4)[:, 0, :]).then_inc(kv_loaded[a], 16)
                sp.dma_start(kv[0:64, a, 2, :], cache[0, b, :, :].rearrange("(r s) n -> r s n", s=16)[:, 0, :]).then_inc(kv_loaded[a], 16)
                sp.dma_start(kv[64:65, a, 2, :], own[b:b + 1, :]).then_inc(kv_loaded[a], 16)
                if n == 0:
                    wait_emptied(sp, ("p", 1, 1))
                    wait_full(sp, ("v", 11, T))
                    sp.dma_start(w_out, w_out_ab[0].rearrange("(k p) n -> p k n", p=P)).then_inc(wout_loaded, 16)
            for l in range(L):
                sp.wait_ge(rows_normed, (2 * l + 1) * (T + 1))
                sp.dma_start(G[:], norm_ffn[l:l + 1, :].to_broadcast([P, D])).then_inc(g_loaded, 16)
                if l == 0:
                    wait_emptied(sp, ("yT", T - 1))
                    sp.wait_ge(stored, stores[0])
                wq = peer_wq[l].rearrange("(k p) n -> p k n", p=P)
                for n in range(KD):
                    if n >= 3:
                        wait_full(sp, ("qs", l, 2 * (n - 3) + 1))
                    sp.dma_start(wq_slot[n % 3], wq[:, :, n * WC:(n + 1) * WC]).then_inc(wq_loaded[n % 3], 16)
                wait_emptied(sp, ("scs", l, HC - 1))
                sp.wait_ge(rows_normed, (2 * l + 2) * (T + 1))
                for h in range(PH):
                    sp.dma_start(sc64[h * B:(h + 1) * B, :], sc_s[0:B, h * 2 * NK:(h + 1) * 2 * NK]).then_inc(sample_moved, 16)
                    sp.dma_start(hrep[h * B:(h + 1) * B, :], Hv[0:B, 0, :]).then_inc(sample_moved, 16)
                if l == 0:
                    sp.wait_ge(acc_done, unit(1, 0))
                    sp.dma_start(G[:], norm_mix[1:2, :].to_broadcast([P, D])).then_inc(g_loaded, 16)
                    sp.dma_start(sk_nat, peer_subkeys[1].rearrange("h c k d -> k (h c) d")).then_inc(sk_loaded, 16)
                    sp.dma_start(poolw, pool_w[0].rearrange("g (k p) n -> p g k n", p=P)).then_inc(pool_loaded, 16)
                    sp.dma_start(pscale, pool_scale[0:1, :].to_broadcast([P, D])).then_inc(pool_loaded, 16)
                    sp.dma_start(pbias, pool_b.rearrange("o g n -> o (g n)").to_broadcast([P, D])).then_inc(pool_loaded, 16)
                    sp.dma_start(pstate[0:B * PS, :], state_pool[0].rearrange("b j n -> (b j) n")).then_inc(pool_loaded, 16)
                    sp.wait_ge(rows_normed, 3 * (T + 1))
                    sp.dma_start(pool_prompt[0, 0, :, :], Hv[P - PS:P, T, :]).then_inc(pool_stored, 16)
                    sp.dma_start(pool_sample[0, :, PS - 1, :], Hv[0:B, 0, :]).then_inc(pool_stored, 16)
                    sp.wait_ge(stored, stores[0])
            sp.wait_ge(rows_normed, 4 * (T + 1))
            sp.dma_start(G[:], norm_final.unsqueeze(0).to_broadcast([P, D])).then_inc(g_loaded, 16)
            for t in range(T):
                sp.wait_ge(rows_normed, 4 * (T + 1) + t + 1)
                store(y_prompt[0, t * P:(t + 1) * P, :], Hv[:, t + 1, :])
            sp.wait_ge(rows_normed, 5 * (T + 1))
            store(y_sample.rearrange("b s d -> (b s) d"), Hv[0:B, 0, :])
            sp.wait_ge(stored, stores[0])
            sp.wait_ge(pool_stored, 32)
            for n in range(2):
                sp.wait_ge(kstage_stored[n], 16 * T // 2)
                sp.wait_ge(cache_copied[n], 16 * B)

        @block.gpsimd
        def _(pool):
            made = [0]

            def step(ins):
                made[0] += 1
                ins.then_inc(pool_consts, 1)
                pool.wait_ge(pool_consts, made[0])

            def keep(ap, base, cm, pattern, fill=0.0, op=ALU.is_ge):
                step(nc.gpsimd.affine_select(out=ap, in_=ap, compare_op=op, fill=fill, base=base,
                                             pattern=pattern, channel_multiplier=cm))

            step(nc.gpsimd.memset(ident[:], 0.0))
            keep(ident[:], 0, 1, [[-1, P]], fill=1.0, op=ALU.not_equal)
            step(nc.gpsimd.iota(dist, pattern=[[-P, T], [-1, P]], base=(T - 1) * P, channel_multiplier=1,
                                allow_small_or_imprecise_dtypes=True))
            step(nc.gpsimd.iota(iota16[:], pattern=[[1, TOP]], base=0, channel_multiplier=0,
                                allow_small_or_imprecise_dtypes=True))
            step(nc.gpsimd.iota(tplus1[:], pattern=[[1, P]], base=1, channel_multiplier=0,
                                allow_small_or_imprecise_dtypes=True))
            step(nc.gpsimd.memset(POOL_CUR[:], 1.0))
            step(nc.gpsimd.memset(POOL_PREV[:], 1.0))
            step(nc.gpsimd.memset(POOL_STATE_M[:], 1.0))
            n = 0
            for src, out in ((state_win_k, win_k_sample), (state_win_v, win_v_sample)):
                for b in range(B):
                    if n >= 2:
                        pool.wait_ge(cache_copied[n % 2], 16 * (n // 2))
                    pool.dma_start(out[0, b, 0:PAST - 1, :].rearrange("r n -> (r n)").rearrange("(a n) -> a n", a=P),
                                   src[0, b, 1:PAST, :].rearrange("r n -> (r n)").rearrange("(a n) -> a n", a=P)
                                   ).then_inc(cache_copied[n % 2], 16)
                    n += 1
                    if n % 2 == 0 and n <= 2 * NG:
                        g = n // 2 - 1
                        w = POOL_W[g]
                        keep(POOL_CUR[:, g, :], 0, -1, [[1, P]])
                        keep(POOL_CUR[:, g, :], w - 1, 1, [[-1, P]])
                        keep(POOL_PREV[:, g, :], w - 1 - P, 1, [[-1, P]])
                        keep(POOL_STATE_M[:, g, :], -(PS + 1 - w), 1, [[-PS, B]])
                        keep(POOL_STATE_M[:, g, :], PS - 1, -1, [[PS, B]])

            def gather(rows, table, landed, st, n, k):
                pool.indirect_dma_start(
                    rows[0:n, k % SLOTS, :], None, table.rearrange("l e d -> (l e) d"),
                    bass.IndirectOffsetOnAxis(ap=idx[0:n, st, k:k + 1], axis=0),
                ).then_inc(landed[k % SLOTS], 16)

            def wait_slots(freed, count):
                pool.wait_ge(freed, count)
                pool.sem_inc(passed, 1)

            def wait_experts(tau):
                pool.wait_ge(idx_ready, tau + 1)
                pool.sem_inc(passed, 1)

            def gather_u(st, tau, n, k):
                if k % 4 == 0:
                    wait_slots(u_freed, tau * TOP + k + 4)
                gather(u_rows, peer_u, u_landed, st, n, k)

            def gather_v(st, tau, n, k):
                if k % 4 == 0:
                    wait_slots(v_freed, tau * TOP + k + 4)
                gather(v_rows, peer_v, v_landed, st, n, k)

            for l in range(L):
                first = task(l, 0, 0)
                wait_experts(first)
                for k in range(TOP):
                    gather_u(first % SETS, first, P, k)
                with pool.Fori(0, T) as i:
                    for h in range(PH):
                        now = task(l, 0, h)
                        wait_experts(i * PH + now + 1)
                        for k in range(TOP):
                            gather_u((now + 1) % SETS, i * PH + now + 1, P, k)
                            gather_v(now % SETS, i * PH + now, P, k)
                for k in range(TOP):
                    gather_v(sample_task(l) % SETS, sample_task(l), PH * B, k)

        @block.tensor
        def _(pe):
            opened = []

            def open_bank(name):
                b, use = JOBS[name]
                assert len(opened) == use * NB + b, name
                opened.append(name)
                if use:
                    pe.wait_ge(bank_emptied[b], use)
                return PSUM[:, b, :]

            def close_bank(ins, name):
                ins.then_inc(bank_full[JOBS[name][0]], 1)

            def transposes(name, width, pieces):
                out = open_bank(name)
                for n, src in enumerate(pieces):
                    rows, cols = src.shape
                    last = nc.tensor.transpose(out[0:cols, n * width:n * width + rows], src, ident[0:rows, 0:rows])
                close_bank(last, name)

            def chunks(row, n=4):
                return [row[:, c * P:(c + 1) * P] for c in range(n)]

            def rows_transposed(key, stage):
                for t in range(T):
                    pe.wait_ge(rows_normed, stage * (T + 1) + t + 1)
                    for half in range(2):
                        transposes((key, t, half), P, chunks(Hv[:, t + 1, half * 512:(half + 1) * 512]))
                pe.wait_ge(rows_normed, (stage + 1) * (T + 1))
                transposes((key, "s"), B, chunks(Hv[0:B, 0, :], KD))

            def wait_rows(key):
                for t in range(T):
                    for half in range(2):
                        wait_emptied(pe, (key, t, half))
                wait_emptied(pe, (key, "s"))

            def subkeys(l):
                pe.wait_ge(sk_loaded, 16 * (l + 1))
                for j in range(4):
                    transposes(("skT", l, j), P, [sk_nat[:, 4 * j + c, :] for c in range(4)])

            def columns(name, lhs, rhs_n):
                for key, lo, n in ((name, 0, SEQ), (rhs_n, SEQ, B)):
                    out = open_bank(key)
                    for k in range(KD):
                        last = nc.tensor.matmul(out[:, 0:n], lhs[:, k, :], HT[:, k, lo:lo + n],
                                                start=(k == 0), stop=(k == KD - 1))
                    close_bank(last, key)

            def queries(l):
                for hc in range(HC):
                    n = hc // 2
                    if hc % 2 == 0:
                        pe.wait_ge(wq_loaded[n % 3], 16 * (l * len(range(n % 3, KD, 3)) + n // 3 + 1))
                    columns(("q", l, hc), wq_slot[n % 3][:, :, (hc % 2) * P:(hc % 2 + 1) * P], ("qs", l, hc))
                    wait_emptied(pe, ("q", l, hc))
                    out = open_bank(("sc", l, hc))
                    for t in range(T):
                        last = nc.tensor.matmul(out[:, t * P:(t + 1) * P], qp[:, hc % 2, t * P:(t + 1) * P],
                                                SKT[:, hc, :], start=True, stop=True)
                    close_bank(last, ("sc", l, hc))
                    wait_emptied(pe, ("qs", l, hc))
                    out = open_bank(("scs", l, hc))
                    close_bank(nc.tensor.matmul(out[0:B, 0:NK], q_s2[:, hc % 2, :], SKT[:, hc, :],
                                                start=True, stop=True), ("scs", l, hc))

            def zero_group(start, done):
                for half in range(2):
                    last = nc.tensor.matmul(PSUM[:, 6 + half, :], zeros[:], COUNT[:, :, :].rearrange("p a b -> p (a b)"),
                                            start=start, stop=not start)
                if done:
                    last.then_inc(acc_done, 1)

            def accumulate(k, tau, n, out_n):
                pe.wait_ge(v_landed[k % SLOTS], tau * 32 + 16 * (k // SLOTS + 1))
                pe.wait_ge(diag_ready, tau * TOP + k + 1)
                for half in range(2):
                    last = nc.tensor.matmul(PSUM[0:out_n, 6 + half, :], diag[0:n, k % DIAGS, 0:out_n],
                                            v_rows[0:n, k % SLOTS, half * 512:(half + 1) * 512],
                                            start=False, stop=False, skip_group_check=True)
                last.then_inc(v_freed, 1)

            pe.wait_ge(consts, 2)
            subkeys(0)
            rows_transposed("hT_mix", 0)
            pe.wait_ge(small_loaded, 32)
            transposes(("conv_state",), 2 * B, chunks(Y[0:2 * B, 0, :]))
            transposes(("conv_w",), 3 * CA, [conv_rows])
            wait_rows("hT_mix")
            for n, ch in enumerate((2, 3, 4, 5, 0, 1, 6, 7, 8, 9)):
                pe.wait_ge(w_loaded[n % 3], 16 * (n // 3 + 1))
                for half in range(2):
                    columns(("p", ch, half), w_in_slot[n % 3][:, :, half * P:(half + 1) * P], ("ps", ch, half))
            for n, ch in ((10, 10), (11, 11)):
                pe.wait_ge(w_loaded[n % 3], 16 * (n // 3 + 1))
                for t in range(T + 1):
                    m = P if t < T else B
                    out = open_bank(("v", ch, t))
                    for k in range(KD):
                        last = nc.tensor.matmul(out[0:m, 0:WC], HT[:, k, t * P:t * P + m], w_in_slot[n % 3][:, k, :],
                                                start=(k == 0), stop=(k == KD - 1))
                    close_bank(last, ("v", ch, t))
            for ch in (8, 9):
                for half in range(2):
                    wait_emptied(pe, ("p", ch, half))
                    wait_emptied(pe, ("ps", ch, half))
            for t in range(T):
                transposes(("kn", t), P, [kT[:, c, t * P:(t + 1) * P] for c in range(CA)])
            transposes(("kns",), P, [kT_s[:, c, :] for c in range(CA)])
            for ch in (6, 7):
                for half in range(2):
                    wait_emptied(pe, ("p", ch, half))
                    wait_emptied(pe, ("ps", ch, half))
            transposes(("qns",), P, [qT_s[:, c, :] for c in range(CA)])
            for ch in (4, 5):
                for half in range(2):
                    wait_emptied(pe, ("p", ch, half))
                    wait_emptied(pe, ("ps", ch, half))
            transposes(("utail",), P, [uT[:, c, SEQ:SEQ + 2] for c in range(CA)])
            transposes(("us",), P, [u_s[:, c, :] for c in range(CA)])

            def scores(m):
                t, h = divmod(m, NH)
                lo = HD * (h % 2)
                out = open_bank(("s", m))
                close_bank(nc.tensor.matmul(out[:, 0:(t + 1) * P], qT[lo:lo + HD, h // 2, t * P:(t + 1) * P],
                                            kT[lo:lo + HD, h // 2, 0:(t + 1) * P], start=True, stop=True), ("s", m))

            def weighted(m):
                t, h = divmod(m, NH)
                wait_emptied(pe, ("pT", m))
                if h == 0 and t >= 2:
                    pe.wait_ge(y_normed, t - 1)
                for kt in range(t + 1):
                    last = nc.tensor.matmul(PSUM[:, 6 + t % 2, h * HD:(h + 1) * HD], PT[:, m % 2, kt * P:(kt + 1) * P],
                                            vn[:, kt, h * HD:(h + 1) * HD], start=(kt == 0), stop=(kt == t))
                last.then_inc(y_done, 1)
                if h == NH - 1:
                    pe.wait_ge(y_normed, t + 1)
                    transposes(("yT", t), P, chunks(Y[:, t % 2, :]))

            for t in range(T):
                for ch in (10, 11):
                    wait_emptied(pe, ("v", ch, t))
            scores(0)
            for m in range(T * NH):
                if m + 1 < T * NH:
                    scores(m + 1)
                pe.wait_ge(probs_ready, m + 1)
                transposes(("pT", m), P, chunks(S[:, m % 2, :], m // NH + 1))
                if m >= 1:
                    weighted(m - 1)
            weighted(T * NH - 1)
            wait_emptied(pe, ("qns",))
            pe.wait_ge(consts, 3)
            for b in range(B):
                out = open_bank(("qrep", b))
                close_bank(nc.tensor.matmul(out[:, :], sel[0:B, b, :], q_s[0:B, :], start=True, stop=True), ("qrep", b))
            pe.wait_ge(k_scored, B)
            out = open_bank(("ssT",))
            for c in range(3):
                last = nc.tensor.transpose(out[0:B * NH, c * P:(c + 1) * P],
                                           S_all[:, c, :, :].rearrange("p b h -> p (b h)"), ident[:])
            close_bank(last, ("ssT",))
            pe.wait_ge(sprobs_ready, 1)
            out = open_bank(("spT",))
            for c in range(3):
                last = nc.tensor.transpose(out[0:LOC[c], c * B * NH:(c + 1) * B * NH],
                                           SP_[0:B * NH, c * P:c * P + LOC[c]], ident[0:B * NH, 0:B * NH])
            close_bank(last, ("spT",))
            wait_emptied(pe, ("spT",))

            def gather_heads(b):
                wait_emptied(pe, ("so", b))
                for c in range(CA):
                    last = nc.tensor.matmul(PSUM[:, 6, c * B + b:c * B + b + 1],
                                            masked[b % 2][0:NH, c * P:(c + 1) * P], ones[0:NH, :], start=True, stop=True)
                last.then_inc(sy_done, 1)

            for b in range(B):
                pe.wait_ge(kv_loaded[b % 2], 64 * (B // 2 + b // 2 + 1))
                out = open_bank(("so", b))
                for c in range(3):
                    last = nc.tensor.matmul(out[0:NH, :], SPT[0:LOC[c], c, b * NH:(b + 1) * NH],
                                            kv[0:LOC[c], b % 2, c, :], start=(c == 0), stop=(c == 2))
                close_bank(last, ("so", b))
                if b:
                    gather_heads(b - 1)
            gather_heads(B - 1)
            pe.wait_ge(wout_loaded, 16)
            for ch in (0, 1):
                for half in range(2):
                    wait_emptied(pe, ("p", ch, half))
                    wait_emptied(pe, ("ps", ch, half))
            for t in range(T + 1):
                m = P if t < T else B
                if t < T:
                    wait_emptied(pe, ("yT", t))
                else:
                    pe.wait_ge(sy_moved, 1)
                for half in range(2):
                    out = open_bank(("wo", t, half))
                    for k in range(KD):
                        last = nc.tensor.matmul(out[0:m, :], yT[:, k, t * P:t * P + m],
                                                w_out[:, k, half * 512:(half + 1) * 512], start=(k == 0), stop=(k == KD - 1))
                    close_bank(last, ("wo", t, half))

            for l in range(L):
                if l == 1:
                    subkeys(1)
                    pe.wait_ge(pool_loaded, 64)
                    for t in range(T):
                        pe.wait_ge(rows_normed, 2 * (T + 1) + t + 1)
                        for half in range(2):
                            out = open_bank(("pp", t, half))
                            for c in range(4):
                                ch = 4 * half + c
                                g = ch * P // GW
                                o_ = out[:, c * P:(c + 1) * P]
                                last = nc.tensor.matmul(o_, Hv[:, t + 1, ch * P:(ch + 1) * P],
                                                        (POOL_CUR if t else POOL_FIRST)[:, g, :], start=True, stop=(t == 0))
                                if t:
                                    last = nc.tensor.matmul(o_, Hv[:, t, ch * P:(ch + 1) * P], POOL_PREV[:, g, :],
                                                            start=False, stop=True)
                            close_bank(last, ("pp", t, half))
                        for half in range(2):
                            wait_emptied(pe, ("pp", t, half))
                            out = open_bank(("pl", t, half))
                            for n in range(2):
                                for k in range(2):
                                    g = 2 * half + n
                                    last = nc.tensor.matmul(out[:, n * GW:(n + 1) * GW], pT[:, t % 2, 2 * g + k, :],
                                                            poolw[:, g, k, :], start=(k == 0), stop=(k == 1))
                            close_bank(last, ("pl", t, half))
                    pe.wait_ge(rows_normed, 3 * (T + 1))
                    out = open_bank(("pps",))
                    for ch in range(KD):
                        g = ch * P // GW
                        o_ = out[:, ch * B:(ch + 1) * B]
                        nc.tensor.matmul(o_, pstate[0:B * PS, ch * P:(ch + 1) * P], POOL_STATE_M[0:B * PS, g, :],
                                         start=True, stop=False)
                        last = nc.tensor.matmul(o_, Hv[0:B, 0, ch * P:(ch + 1) * P], POOL_NEW_M[0:B, g, :],
                                                start=False, stop=True)
                    close_bank(last, ("pps",))
                    wait_emptied(pe, ("pps",))
                    for half in range(2):
                        out = open_bank(("pl", T, half))
                        for n in range(2):
                            for k in range(2):
                                g = 2 * half + n
                                last = nc.tensor.matmul(out[0:B, n * GW:(n + 1) * GW], pT_s[:, 2 * g + k, :],
                                                        poolw[:, g, k, :], start=(k == 0), stop=(k == 1))
                        close_bank(last, ("pl", T, half))
                for j in range(4):
                    wait_emptied(pe, ("skT", l, j))
                rows_transposed(f"hT_ffn{l}", 2 * l + 1)
                wait_rows(f"hT_ffn{l}")
                queries(l)
                if l == 0:
                    pe.sem_inc(v_freed, SLOTS)
                else:
                    pe.wait_ge(acc_added, unit(l, 0))
                zero_group(True, False)
                zero_group(False, True)
                with pe.Fori(0, T) as i:
                    pe.wait_ge(acc_added, i + unit(l, 1))
                    zero_group(True, False)
                    for h in range(PH):
                        for k in range(TOP):
                            accumulate(k, i * PH + task(l, 0, h), P, P)
                    zero_group(False, True)
                pe.wait_ge(acc_added, unit(l, T + 1))
                zero_group(True, False)
                for k in range(TOP):
                    accumulate(k, sample_task(l), PH * B, B)
                zero_group(False, True)
            assert len(opened) == len(JOBS)

        @block.scalar
        def _(act):
            def copy_out(name, out, src, scale=1.0):
                wait_full(act, name)
                emptied(nc.scalar.activation(out, src, ACT.Copy, scale=scale), name)

            def wide(name, n=4, width=P):
                return bank(name)[:, 0:n * width].rearrange("p (c n) -> p c n", c=n)

            def rows_transposed(key):
                for t in range(T):
                    for half in range(2):
                        copy_out((key, t, half), HT[:, 4 * half:4 * half + 4, t * P:(t + 1) * P], wide((key, t, half)))
                copy_out((key, "s"), HT[:, :, SEQ:SEQ + B], wide((key, "s"), KD, B))

            def root(stage):
                act.wait_ge(squares_ready, stage + 1)
                nc.scalar.activation(rstd[:], ss[:], ACT.Sqrt).then_inc(root_ready, 1)

            def subkeys(l):
                for j in range(4):
                    copy_out(("skT", l, j), SKT[:, 4 * j:4 * j + 4, :], wide(("skT", l, j)))

            def queries(l):
                for hc in range(HC):
                    if hc >= 2:
                        wait_full(act, ("scs", l, hc - 2))
                    copy_out(("q", l, hc), qp[:, hc % 2, :], bank(("q", l, hc)))
                    copy_out(("qs", l, hc), q_s2[:, hc % 2, :], bank(("qs", l, hc))[:, 0:B])

            def gates(par, tau):
                act.wait_ge(cs_ready, tau + 1)
                nc.scalar.activation(ex[:, par, :], cs[:, par, :], ACT.Exp, bias=ncs[:, par:par + 1],
                                     accum_out=exsum[:, par:par + 1]).then_inc(gates_exp, 1)

            def experts(par, tau, n, selector, out_n):
                act.wait_ge(u_freed, tau * TOP + TOP + SLOTS)
                nc.scalar.activation(act_h[0:n, par, :], dots[0:n, par, :], ACT.Gelu).then_inc(gelu_done, 1)
                act.wait_ge(gate_ready, tau + 1)
                for k in range(TOP):
                    act.wait_ge(v_freed, tau * TOP + k + 1 + SLOTS - DIAGS)
                    nc.scalar.activation(diag[0:n, k % DIAGS, 0:out_n], selector, ACT.Copy,
                                         scale=gate[0:n, par, k:k + 1]).then_inc(diag_ready, 1)

            root(0)
            subkeys(0)
            rows_transposed("hT_mix")
            for ch in (2, 3, 6, 7, 8, 9):
                for half in range(2):
                    c = ch * 2 % 4 + half
                    big, small, scale = {1: (cT, c_s, 1.0), 3: (qT, qT_s, HD ** -0.5), 4: (kT, kT_s, 1.0)}[ch // 2]
                    copy_out(("p", ch, half), big[:, c, :], bank(("p", ch, half)), scale)
                    copy_out(("ps", ch, half), small[:, c, :], bank(("ps", ch, half))[:, 0:B], scale)
            for ch in (10, 11):
                lo = (ch - 10) * WC
                for t in range(T):
                    copy_out(("v", ch, t), vn[:, t, lo:lo + WC], bank(("v", ch, t))[:, 0:WC])
                copy_out(("v", ch, T), v_s[0:B, lo:lo + WC], bank(("v", ch, T))[0:B, 0:WC])
            for t in range(T):
                if t >= 2:
                    act.wait_ge(kstage_stored[t % 2], 16 * (t // 2))
                copy_out(("kn", t), kstage[:, t % 2, :], bank(("kn", t)))
            copy_out(("kns",), k_s[0:B, :], bank(("kns",))[0:B, :])
            copy_out(("qns",), q_s[0:B, :], bank(("qns",))[0:B, :])
            copy_out(("utail",), utail[0:2, :], bank(("utail",))[0:2, :])
            copy_out(("us",), unew[0:B, :], bank(("us",))[0:B, :])
            for m in range(T * NH):
                t = m // NH
                n = (t + 1) * P
                act.wait_ge(max_ready, m + 1)
                nc.scalar.activation(S[:, m % 2, 0:n], S[:, m % 2, 0:n], ACT.Exp,
                                     bias=negm[:, m % 2:m % 2 + 1]).then_inc(exp_ready, 1)
                if m >= 1:
                    tp = (m - 1) // NH
                    if m - 1 >= 2:
                        act.wait_ge(y_done, m - 2)
                    copy_out(("pT", m - 1), PT[:, (m - 1) % 2, 0:(tp + 1) * P], bank(("pT", m - 1))[:, 0:(tp + 1) * P])
                if m >= 2 and (m - 2) % NH == NH - 1:
                    tt = (m - 2) // NH
                    copy_out(("yT", tt), yT[:, CA:2 * CA, tt * P:(tt + 1) * P], wide(("yT", tt)))
            m = T * NH
            act.wait_ge(y_done, m - 2)
            copy_out(("pT", m - 1), PT[:, (m - 1) % 2, :], bank(("pT", m - 1)))
            copy_out(("yT", T - 1), yT[:, CA:2 * CA, (T - 1) * P:T * P], wide(("yT", T - 1)))
            act.wait_ge(smax_ready, 1)
            nc.scalar.activation(SP_[0:B * NH, :], bank(("ssT",))[0:B * NH, 0:2 * P + SAMPLE_ROWS], ACT.Exp,
                                 bias=negm[0:B * NH, 0:1]).then_inc(sexp_ready, 1)
            for l in range(L):
                if l == 1:
                    root(2)
                    subkeys(1)
                    for t in range(T):
                        if t >= 2:
                            wait_full(act, ("pl", t - 2, 1))
                        for half in range(2):
                            copy_out(("pp", t, half), pT[:, t % 2, 4 * half:4 * half + 4, :], wide(("pp", t, half)))
                    copy_out(("pps",), pT_s[:, :, :], wide(("pps",), KD, B))
                root(2 * l + 1)
                rows_transposed(f"hT_ffn{l}")
                queries(l)
                gates(task(l, 0, 0) % SETS, task(l, 0, 0))
                with act.Fori(0, T) as i:
                    for h in range(PH):
                        now = task(l, 0, h)
                        gates((now + 1) % SETS, i * PH + now + 1)
                        experts(now % SETS, i * PH + now, P, ident[:], P)
                experts(sample_task(l) % SETS, sample_task(l), PH * B, sel64[0:PH * B, :], B)
            root(4)

        @block.vector
        def _(dve):
            chain = {"sem": dve_chain, "n": 0}

            def step(ins):
                chain["n"] += 1
                ins.then_inc(chain["sem"], 1)
                dve.wait_ge(chain["sem"], chain["n"])

            def begin_loop():
                chain["static"] = chain["n"]
                chain["sem"], chain["n"] = dve_loop, 0

            def end_body():
                dve.sem_clear(dve_loop)
                chain["n"] = 0

            def end_loop():
                chain["sem"], chain["n"] = dve_chain, chain["static"]

            V = nc.vector

            def norm(stage):
                slots = [(t + 1, P) for t in range(T)] + [(0, B)]
                last = None
                for s, n in slots:
                    chain["n"] += 1
                    V.tensor_tensor_reduce(out=Hv[0:n, s, :], in0=X[0:n, s, :], in1=X[0:n, s, :], scale=1.0,
                                           scalar=0.0, op0=ALU.mult, op1=ALU.add,
                                           accum_out=ss[0:n, s:s + 1]).then_inc(dve_chain, 1)
                dve.wait_ge(dve_chain, chain["n"])
                V.tensor_scalar(ss[:], ss[:], 1.0 / D, EPS, ALU.mult, ALU.add).then_inc(squares_ready, 1)
                dve.wait_ge(root_ready, stage + 1)
                step(V.reciprocal(rstd[:], rstd[:]))
                dve.wait_ge(g_loaded, 16 * (stage + 1))
                for s, n in slots:
                    V.scalar_tensor_tensor(out=Hv[0:n, s, :], in0=X[0:n, s, :], scalar=rstd[0:n, s:s + 1],
                                           in1=G[0:n, :], op0=ALU.mult, op1=ALU.mult).then_inc(rows_normed, 1)

            V.memset(X[:, 0, :], 0.0).then_inc(consts, 1)
            step(V.memset(zeros[:], 0.0))
            step(V.memset(ss[:], 1.0))
            step(V.memset(ones[:], 1.0))
            step(V.memset(sc64[:], 0.0))
            step(V.memset(uT[:, :, 0:2], 0.0))
            dve.wait_ge(pool_consts, 8)
            t0 = S[:, 0, :].rearrange("p (a b) -> p a b", a=T)
            t1 = S[:, 1, :].rearrange("p (a b) -> p a b", a=T)
            t2 = PT[:, 0, :].rearrange("p (a b) -> p a b", a=T)
            ti = PT[:, 1, :].rearrange("p (a b) -> p a b", a=T).bitcast(i32)
            step(V.tensor_scalar(t0, dist, 128, None, ALU.is_le))
            for mask in (3, 15):
                step(V.tensor_scalar(ti, dist, mask, None, ALU.bitwise_and))
                step(V.tensor_scalar(t1, ti, 0, None, ALU.is_equal))
                step(V.tensor_tensor(t0, t0, t1, ALU.add))
            step(V.tensor_scalar(t2, dist, 0, None, ALU.is_ge))
            step(V.tensor_tensor(COUNT[:], t0, t2, ALU.mult))
            step(V.tensor_scalar(MASKED[:], COUNT[:], 0.0, NEG, ALU.is_equal, ALU.mult))
            step(V.tensor_reduce(sel64[0:PH * B, :], ident[0:PH * B, 0:PH * B].rearrange("p (h b) -> p b h", b=B),
                                 AX.X, ALU.add))
            step(V.memset(rden[:], 0.0))
            V.memset(den[:], 0.0).then_inc(consts, 1)
            step(V.tensor_copy(sel[0:B, :, :], ident[0:B, 0:B].unsqueeze(2).to_broadcast([B, B, P])))
            V.memset(negm[:], 0.0).then_inc(consts, 1)
            dve.wait_ge(consts, 3)
            dve.wait_ge(x_loaded, 16 * (T + 1))
            norm(0)
            dve.wait_ge(small_loaded, 32)
            wait_full(dve, ("conv_state",))
            emptied(V.tensor_copy(conv_st[:, :, :, :].rearrange("p c b j -> p (c b j)"),
                                  bank(("conv_state",))[:, 0:CA * 2 * B]), ("conv_state",))
            wait_full(dve, ("conv_w",))
            emptied(V.tensor_copy(convw[:, :, :].rearrange("p i c -> p (i c)"), bank(("conv_w",))[:, 0:3 * CA]),
                    ("conv_w",))
            wait_emptied(dve, ("conv_state",))
            wait_emptied(dve, ("conv_w",))
            for t in range(T):
                for half in range(2):
                    wait_full(dve, ("hT_mix", t, half))
            wait_full(dve, ("hT_mix", "s"))
            V.memset(H[:, 0:2 * KV], 0.0).then_inc(kv_cleared, 1)
            for ch in (4, 5):
                for half in range(2):
                    c = (ch - 4) * 2 + half
                    wait_emptied(dve, ("p", ch - 2, half))
                    wait_emptied(dve, ("ps", ch - 2, half))
                    wait_full(dve, ("p", ch, half))
                    emptied(V.tensor_tensor(uT[:, c, 2:UW], bank(("p", ch, half)), cT[:, c, :], ALU.mult), ("p", ch, half))
                    wait_full(dve, ("ps", ch, half))
                    emptied(V.tensor_tensor(u_s[:, c, :], bank(("ps", ch, half))[:, 0:B], c_s[:, c, :], ALU.mult),
                            ("ps", ch, half))
            for ch in (0, 1):
                for half in range(2):
                    c = ch * 2 + half
                    wait_emptied(dve, ("p", ch + 4, half))
                    wait_emptied(dve, ("ps", ch + 4, half))
                    y, ys = yT[:, c, 0:SEQ], yT[:, c, SEQ:HT_N]
                    step(V.tensor_scalar(y, uT[:, c, 0:SEQ], convw[:, 0, c:c + 1], None, ALU.mult))
                    step(V.tensor_scalar(ys, conv_st[:, c, :, 0], convw[:, 0, c:c + 1], None, ALU.mult))
                    step(V.scalar_tensor_tensor(out=y, in0=uT[:, c, 1:SEQ + 1], scalar=convw[:, 1, c:c + 1], in1=y,
                                                op0=ALU.mult, op1=ALU.add))
                    step(V.scalar_tensor_tensor(out=ys, in0=conv_st[:, c, :, 1], scalar=convw[:, 1, c:c + 1], in1=ys,
                                                op0=ALU.mult, op1=ALU.add))
                    step(V.scalar_tensor_tensor(out=y, in0=uT[:, c, 2:UW], scalar=convw[:, 2, c:c + 1], in1=y,
                                                op0=ALU.mult, op1=ALU.add))
                    step(V.scalar_tensor_tensor(out=ys, in0=u_s[:, c, :], scalar=convw[:, 2, c:c + 1], in1=ys,
                                                op0=ALU.mult, op1=ALU.add))
                    wait_full(dve, ("p", ch, half))
                    emptied(V.tensor_tensor(y, bank(("p", ch, half)), y, ALU.mult), ("p", ch, half))
                    wait_full(dve, ("ps", ch, half))
                    emptied(V.tensor_tensor(ys, bank(("ps", ch, half))[:, 0:B], ys, ALU.mult), ("ps", ch, half))

            def masked_scores(m):
                t = m // NH
                n = (t + 1) * P
                if m >= 2:
                    wait_full(dve, ("pT", m - 2))
                wait_full(dve, ("s", m))
                emptied(V.tensor_tensor(S[:, m % 2, 0:n], bank(("s", m))[:, 0:n],
                                        MASKED[:, T - 1 - t:T, :].rearrange("p a b -> p (a b)"), ALU.add), ("s", m))
                wait_emptied(dve, ("s", m))
                step(V.tensor_reduce(negm[:, m % 2:m % 2 + 1], S[:, m % 2, 0:n], AX.X, ALU.max))
                V.tensor_scalar(negm[:, m % 2:m % 2 + 1], negm[:, m % 2:m % 2 + 1], -1.0, None, ALU.mult).then_inc(max_ready, 1)

            def counted(m):
                t, h = divmod(m, NH)
                n = (t + 1) * P
                dve.wait_ge(exp_ready, m + 1)
                V.tensor_tensor_reduce(out=S[:, m % 2, 0:n], in0=S[:, m % 2, 0:n],
                                       in1=COUNT[:, T - 1 - t:T, :].rearrange("p a b -> p (a b)"), scale=1.0, scalar=0.0,
                                       op0=ALU.mult, op1=ALU.add, accum_out=den[:, t % 2, h:h + 1]).then_inc(probs_ready, 1)

            def normed(t):
                dve.wait_ge(probs_ready, (t + 1) * NH)
                step(V.reciprocal(rden[:, t % 2, :], den[:, t % 2, :]))
                dve.wait_ge(y_done, (t + 1) * NH)
                if t >= 2:
                    wait_full(dve, ("yT", t - 2))
                V.tensor_tensor(Y[:, t % 2, :].rearrange("p (h d) -> p h d", h=NH),
                                PSUM[:, 6 + t % 2, :].rearrange("p (h d) -> p h d", h=NH),
                                rden[:, t % 2, :].unsqueeze(2).to_broadcast([P, NH, HD]), ALU.mult).then_inc(y_normed, 1)

            masked_scores(0)
            for m in range(T * NH):
                if m + 1 < T * NH:
                    masked_scores(m + 1)
                counted(m)
                if m >= 1 and (m - 1) % NH == NH - 1:
                    normed((m - 1) // NH)
            normed(T - 1)
            dve.wait_ge(y_normed, T)
            wait_full(dve, ("yT", T - 1))
            wait_full(dve, ("yT", T - 2))
            for b in range(B):
                dve.wait_ge(kv_loaded[b % 2], 64 * (b // 2 + 1))
                wait_full(dve, ("qrep", b))
                if b:
                    dve.wait_ge(k_scored, b)
                emptied(V.tensor_tensor(prod.rearrange("p (t n) -> p t n", t=3), kv[:, b % 2, :, :],
                                        bank(("qrep", b)).unsqueeze(1).to_broadcast([P, 3, DA]), ALU.mult), ("qrep", b))
                wait_emptied(dve, ("qrep", b))
                V.tensor_reduce(S_all[:, :, b, :], prod.rearrange("p (t h d) -> p t h d", t=3, h=NH), AX.X,
                                ALU.add).then_inc(k_scored, 1)
            R = B * NH
            NS = 2 * P + SAMPLE_ROWS
            wait_full(dve, ("ssT",))
            step(V.tensor_reduce(negm[0:R, 0:1], bank(("ssT",))[0:R, 0:NS], AX.X, ALU.max))
            V.tensor_scalar(negm[0:R, 0:1], negm[0:R, 0:1], -1.0, None, ALU.mult).then_inc(smax_ready, 1)
            dve.wait_ge(sexp_ready, 1)
            emptied(V.tensor_scalar(SP_[0:R, NS - 1:NS], SP_[0:R, NS - 1:NS], 3.0, None, ALU.mult), ("ssT",))
            wait_emptied(dve, ("ssT",))
            step(V.tensor_reduce(den[0:R, 0, 0:1], SP_[0:R, 0:NS], AX.X, ALU.add))
            step(V.reciprocal(rden[0:R, 0, 0:1], den[0:R, 0, 0:1]))
            V.tensor_scalar(SP_[0:R, 0:NS], SP_[0:R, 0:NS], rden[0:R, 0, 0:1], None, ALU.mult).then_inc(sprobs_ready, 1)
            wait_full(dve, ("spT",))
            for c in range(3):
                ins = V.tensor_copy(SPT[0:LOC[c], c, :], bank(("spT",))[0:LOC[c], c * R:(c + 1) * R])
                if c < 2:
                    step(ins)
            emptied(ins, ("spT",))
            for b in range(B):
                wait_full(dve, ("so", b))
                if b >= 2:
                    dve.wait_ge(sy_done, b - 1)
                emptied(V.tensor_tensor(masked[b % 2][0:NH, :].rearrange("p (h d) -> p h d", h=NH),
                                        bank(("so", b))[0:NH, :].rearrange("p (h d) -> p h d", h=NH),
                                        ident[0:NH, 0:NH].unsqueeze(2).to_broadcast([NH, NH, HD]), ALU.mult), ("so", b))
            dve.wait_ge(sy_done, B)
            V.tensor_copy(yT[:, CA:2 * CA, SEQ:HT_N],
                          PSUM[:, 6, 0:CA * B].rearrange("p (c b) -> p c b", c=CA)).then_inc(sy_moved, 1)
            for t in range(T + 1):
                s, n = (t + 1, P) if t < T else (0, B)
                for half in range(2):
                    wait_full(dve, ("wo", t, half))
                    cols = slice(half * 512, (half + 1) * 512)
                    emptied(V.tensor_tensor(X[0:n, s, cols], bank(("wo", t, half))[0:n, :], X[0:n, s, cols], ALU.add),
                            ("wo", t, half))
            for t in range(T + 1):
                for half in range(2):
                    wait_emptied(dve, ("wo", t, half))

            def search(part, src, st, offset):
                sums = cand.rearrange("p (a b) -> p a b", a=TOP)
                if part == 0:
                    step(V.tensor_copy(sc.rearrange("p c k -> p (c k)"), src))
                    step(V.max(sv[:, 0, 0:8], sc[:, 0, :]))
                if part == 1:
                    step(V.max_index(si[:, 0, 0:8], sv[:, 0, 0:8], sc[:, 0, :]))
                    step(V.match_replace(scw[:, 0, :], sv[:, 0, 0:8], sc[:, 0, :], LOWEST))
                if part == 2:
                    step(V.max(sv[:, 0, 8:16], scw[:, 0, :]))
                    step(V.max_index(si[:, 0, 8:16], sv[:, 0, 8:16], scw[:, 0, :]))
                if part == 3:
                    step(V.max(sv[:, 1, 0:8], sc[:, 1, :]))
                    step(V.max_index(si[:, 1, 0:8], sv[:, 1, 0:8], sc[:, 1, :]))
                if part == 4:
                    step(V.match_replace(scw[:, 1, :], sv[:, 1, 0:8], sc[:, 1, :], LOWEST))
                    step(V.max(sv[:, 1, 8:16], scw[:, 1, :]))
                if part == 5:
                    step(V.max_index(si[:, 1, 8:16], sv[:, 1, 8:16], scw[:, 1, :]))
                    step(V.tensor_tensor(sums, sv[:, 0, :].unsqueeze(2).to_broadcast([P, TOP, TOP]),
                                         sv[:, 1, :].unsqueeze(1).to_broadcast([P, TOP, TOP]), ALU.add))
                if part == 6:
                    step(V.max(cs[:, st, 0:8], cand))
                    step(V.max_index(ci[:, 0:8], cs[:, st, 0:8], cand))
                if part == 7:
                    step(V.match_replace(candw, cs[:, st, 0:8], cand, LOWEST))
                    step(V.max(cs[:, st, 8:16], candw))
                if part == 8:
                    V.tensor_scalar(ncs[:, st:st + 1], cs[:, st, 0:1], -1.0, None, ALU.mult).then_inc(cs_ready, 1)
                    step(V.max_index(ci[:, 8:16], cs[:, st, 8:16], candw))
                if part == 9:
                    step(V.tensor_scalar(cij[:, 0, :], ci[:], 4, None, ALU.logical_shift_right))
                    step(V.tensor_scalar(cij[:, 1, :], ci[:], TOP - 1, None, ALU.bitwise_and))
                    step(V.tensor_copy(cijf[:], cij[:]))
                if part == 10:
                    step(V.tensor_copy(sif[:], si[:]))
                    step(V.tensor_tensor(onehot[:], cijf[:].unsqueeze(3).to_broadcast([P, 2, TOP, TOP]),
                                         iota16[:].unsqueeze(1).unsqueeze(1).to_broadcast([P, 2, TOP, TOP]), ALU.is_equal))
                if part == 11:
                    step(V.tensor_tensor(onehot[:], onehot[:], sif[:].unsqueeze(2).to_broadcast([P, 2, TOP, TOP]), ALU.mult))
                if part == 12:
                    step(V.tensor_reduce(picked[:], onehot[:], AX.X, ALU.add))
                    step(V.tensor_scalar(picked[:, 0, :], picked[:, 0, :], float(NK), float(offset), ALU.mult, ALU.add))
                if part == 13:
                    V.tensor_tensor(idx[:, st, :], picked[:, 0, :], picked[:, 1, :], ALU.add).then_inc(idx_ready, 1)

            def product(st, tau, n, row, k):
                s = k % SLOTS
                dve.wait_ge(u_landed[s], tau * 32 + 16 * (k // SLOTS + 1))
                V.tensor_tensor_reduce(out=u_rows[0:n, s, :], in0=u_rows[0:n, s, :], in1=row, scale=1.0, scalar=0.0,
                                       op0=ALU.mult, op1=ALU.add,
                                       accum_out=dots[0:n, st, k:k + 1]).then_inc(u_freed, 1)

            def weigh(par, tau, n):
                dve.wait_ge(gates_exp, tau + 1)
                step(V.reciprocal(rsum[0:n, :], exsum[0:n, par:par + 1]))
                dve.wait_ge(gelu_done, tau + 1)
                V.scalar_tensor_tensor(out=gate[0:n, par, :], in0=ex[0:n, par, :], scalar=rsum[0:n, :],
                                       in1=act_h[0:n, par, :], op0=ALU.mult, op1=ALU.mult).then_inc(gate_ready, 1)

            def add_unit(units, row, n=P):
                dve.wait_ge(acc_done, units)
                step(V.tensor_tensor(row[:, 0:512], PSUM[0:n, 6, :], row[:, 0:512], ALU.add))
                V.tensor_tensor(row[:, 512:D], PSUM[0:n, 7, :], row[:, 512:D], ALU.add).then_inc(acc_added, 1)

            Xf = X[:, :, :].rearrange("p s d -> p (s d)")
            for l in range(L):
                if l == 1:
                    dve.wait_ge(pool_consts, POOL_STEPS)
                    for g, w in enumerate(POOL_W):
                        step(V.tensor_scalar(onehot_row, tplus1[:], float(w), None, ALU.min))
                        step(V.reciprocal(onehot_row, onehot_row))
                        step(V.tensor_tensor(POOL_FIRST[:, g, :], POOL_CUR[:, g, :], onehot_row, ALU.mult))
                        step(V.tensor_tensor(POOL_FIRST[:, g, :], POOL_FIRST[:, g, :], ident[:], ALU.subtract))
                        step(V.tensor_scalar(POOL_CUR[:, g, :], POOL_CUR[:, g, :], 1.0 / w, None, ALU.mult))
                        step(V.tensor_tensor(POOL_CUR[:, g, :], POOL_CUR[:, g, :], ident[:], ALU.subtract))
                        step(V.tensor_scalar(POOL_PREV[:, g, :], POOL_PREV[:, g, :], 1.0 / w, None, ALU.mult))
                        step(V.tensor_scalar(POOL_STATE_M[:, g, :], POOL_STATE_M[:, g, :], 1.0 / w, None, ALU.mult))
                        step(V.tensor_scalar(POOL_NEW_M[:, g, :], ident[:, 0:B], 1.0 / w - 1.0, None, ALU.mult))
                    norm(2)
                    for t in range(T + 1):
                        s, n = (t + 1, P) if t < T else (0, B)
                        for half in range(2):
                            wait_full(dve, ("pl", t, half))
                            if t == 0 and half == 0:
                                dve.wait_ge(pool_loaded, 64)
                            cols = slice(half * 512, (half + 1) * 512)
                            tmp = hcur[0:n, cols]
                            emptied(V.tensor_tensor(tmp, bank(("pl", t, half))[0:n, :], pbias[0:n, cols], ALU.add),
                                    ("pl", t, half))
                            wait_emptied(dve, ("pl", t, half))
                            step(V.tensor_tensor(tmp, tmp, pscale[0:n, cols], ALU.mult))
                            step(V.tensor_tensor(X[0:n, s, cols], X[0:n, s, cols], tmp, ALU.add))
                    dve.wait_ge(pool_stored, 32)
                norm(2 * l + 1)
                for hc in range(HC):
                    wait_full(dve, ("sc", l, hc))
                    emptied(V.tensor_copy(SCt[:, :, hc, :], bank(("sc", l, hc)).rearrange("p (t k) -> p t k", t=T)),
                            ("sc", l, hc))
                    wait_full(dve, ("scs", l, hc))
                    emptied(V.tensor_copy(sc_s[0:B, hc * NK:(hc + 1) * NK], bank(("scs", l, hc))[0:B, 0:NK]),
                            ("scs", l, hc))
                for hc in range(HC):
                    wait_emptied(dve, ("sc", l, hc))
                    wait_emptied(dve, ("scs", l, hc))
                dve.wait_ge(sample_moved, 256 * (l + 1))
                if l == 0:
                    for n in range(2):
                        dve.wait_ge(kstage_stored[n], 16 * T // 2)
                    dve.sem_inc(u_freed, SLOTS)
                NT = 2 * NK
                t0_ = task(l, 0, 0)
                for part in range(TOP):
                    search(part, SC[:, 0:NT], t0_ % SETS, l * NE)
                begin_loop()
                with dve.Fori(0, T) as i:
                    step(V.tensor_copy(hcur[:], H[:, bass.ds((i + 1) * D, D)]))
                    for h in range(PH):
                        now = task(l, 0, h)
                        tau = i * PH + now
                        for k in range(TOP):
                            product(now % SETS, tau, P, hcur[:], k)
                            search(k, SC[:, bass.ds((i * PH + h + 1) * NT, NT)], (now + 1) % SETS, l * NE)
                        if h == 0:
                            dve.wait_ge(acc_done, i + unit(l, 1))
                            step(V.tensor_tensor(Xf[:, bass.ds(i * D, 512)], Xf[:, bass.ds(i * D, 512)], PSUM[:, 6, :], ALU.add))
                            V.tensor_tensor(Xf[:, bass.ds(i * D + 512, 512)], Xf[:, bass.ds(i * D + 512, 512)],
                                            PSUM[:, 7, :], ALU.add).then_inc(acc_added, 1)
                        weigh(now % SETS, tau, P)
                    end_body()
                end_loop()
                tau = sample_task(l)
                for k in range(TOP):
                    product(tau % SETS, tau, PH * B, hrep[0:PH * B, :], k)
                add_unit(unit(l, T + 1), X[:, T, :])
                weigh(tau % SETS, tau, PH * B)
                add_unit(unit(l, T + 2), X[0:B, 0, :], B)
                dve.wait_ge(acc_added, unit(l, T + 2))
            norm(4)


_INS = ["x_prompt", "x_sample", "state_conv", "state_win_k", "state_win_v", "state_pool", "norm_mix", "w_in_ab",
        "conv_w", "w_out_ab", "pool_w", "pool_b", "pool_scale", "norm_ffn", "peer_wq", "peer_subkeys", "peer_u",
        "peer_v", "norm_final"]
_OUTS = [("y_prompt", (1, SEQ, D)), ("y_sample", (B, 1, D)), ("conv_prompt", (1, 1, 2, DA)),
         ("conv_sample", (1, B, 2, DA)), ("win_k_prompt", (1, SEQ, DA)), ("win_k_sample", (1, B, PAST, DA)),
         ("win_v_prompt", (1, SEQ, DA)), ("win_v_sample", (1, B, PAST, DA)),
         ("pool_prompt", (1, 1, PS, D)), ("pool_sample", (1, B, PS, D))]


def kernel(**inputs):
    import numpy as _np
    import concourse.bacc as _bacc
    from concourse.bass_utils import run_bass_kernel_spmd as _run

    nc = _bacc.Bacc("TRN2", target_bir_lowering=False, num_devices=1)
    arrays, args = {}, []
    for name in _INS:
        a = _np.ascontiguousarray(inputs[name])
        if name in ("state_win_k", "state_win_v"):
            a = a.reshape(1, B, PAST, DA)
        arrays[f"in_{name}"] = a
        args.append(nc.dram_tensor(f"in_{name}", a.shape, mybir.dt.from_np(a.dtype), kind="ExternalInput").ap())
    for name, shape in _OUTS:
        args.append(nc.dram_tensor(f"out_{name}", shape, f32, kind="ExternalOutput").ap())
    build(nc, *args)
    r = _run(nc, [arrays], core_ids=[0])
    out = {name: r.results[0][f"out_{name}"] for name, _ in _OUTS}
    for name in ("win_k_prompt", "win_v_prompt"):
        out[name] = out[name].reshape(1, 1, SEQ, NH, HD)
    for name in ("win_k_sample", "win_v_sample"):
        out[name] = out[name].reshape(1, B, PAST, NH, HD)
    return tuple(out[name] for name, _ in _OUTS)
```

```python
import concourse.bass as bass
from concourse import mybir
from concourse.alu_op_type import AluOpType as ALU
from contextlib import ExitStack

f32 = mybir.dt.float32
u32 = mybir.dt.uint32
i32 = mybir.dt.int32
ACT = mybir.ActivationFunctionType
AX = mybir.AxisListType

P = 128
D = 1024
KD = D // P
SEQ = 512
T = SEQ // P
B = 8
L = 2
NH = 8
HD = 64
DA = NH * HD
CA = DA // P
PAST = 1024
PH = 8
HC = 2 * PH
NK = 128
NE = NK * NK
TOP = 16
EPS = 1e-6
NEG = -1e30
LOWEST = -3.0e38
POOL_W = (2, 4, 8, 16)
NG = len(POOL_W)
GW = D // NG
PS = max(POOL_W) - 1
WC = P
NW = 3
BT = T // 2
BN = BT * P
HT_N = BN + B
NB = 5
U_SLOTS = 4
V_SLOTS = 8
DIAGS = 4
SETS = 4
SAMPLE_ROWS = 65
LOC = (P, P, SAMPLE_ROWS)
TASKS = T * PH + 1
NORMS = ((1, 2, 0), (1, 2, 0), (3, 4), (3, 4), (1, 2), (1, 2), (3, 4, 0), (3, 4, 0), (1, 2, 3, 4), (0,))


def has_sample(l, b):
    return (l, b) in ((0, 0), (1, 1))


def pieces(l, b):
    out = []
    e = 4 * l + 2 * b

    def norm(e):
        out.extend([(("squares", e), 2), (("normed", e), 2)])

    def transposed(e):
        for j in range(BT):
            for half in range(2):
                out.append((("hT", e, j, half), 1))
        if has_sample(l, b):
            out.append((("hT", e, "s", 0), 1))

    norm(e)
    if l == 0:
        transposed(e)
        if b == 0:
            out.append((("small",), 1))
        for kind in "cxbqk":
            for c in range(CA):
                out.append((("p", b, kind, c), 2.8))
        for c in range(CA):
            out.append((("v", b, c), 2.8))
        for j in range(BT):
            out.append((("kn", b, j), 1))
        out.append((("tails", b), 1))
        out.append((("attend", b, -1), 1))
        for m in range(BT * NH):
            out.append((("attend", b, m), 1.6))
        out.append((("attend", b, BT * NH), 2))
        if b == 0:
            out.append((("sample",), 1))
        for c in range(KD):
            out.append((("wo", b, c), 2.8))
    else:
        for j in range(BT):
            for half in range(2):
                out.append((("pp", b, j, half), 2))
        if b == 1:
            out.append((("pps",), 3))
        for j in range(BT):
            for half in range(2):
                out.append((("pl", b, j, half), 3))
        if b == 1:
            out.extend([(("pl", b, BT, 0), 2), (("pl", b, BT, 1), 2)])
        out.append((("mixed", b), 2))
    if b == 0:
        for j in range(4):
            out.append((("skT", l, j), 1))
    norm(e + 1)
    transposed(e + 1)
    out.append((("q", l, b, 0), 3))
    for hc in range(HC):
        if hc + 1 < HC:
            out.append((("q", l, b, hc + 1), 2.8))
        out.append((("sc", l, b, hc), 0.2))
    out.append((("scored", l, b), 1))
    return out


def agenda():
    found = {}
    for l, b, start, end in ((0, 1, 0, 14 * TOP), (1, 0, 16 * TOP, 31 * TOP), (1, 1, TASKS * TOP, 47 * TOP)):
        todo = pieces(l, b)
        scale = min(1.6, (end - start - 2) / sum(n for _, n in todo))
        at = float(start)
        for piece, n in todo:
            found.setdefault(int(at), []).append(piece)
            at += n * scale
        assert at <= end
    return found


AGENDA = agenda()


def jobs_of(piece):
    kind = piece[0]
    if kind in ("hT", "p", "v", "kn", "wo", "skT", "pp", "pps", "pl", "q", "sc"):
        return [piece]
    if kind == "small":
        return [("conv_state",), ("conv_w",)]
    if kind == "tails":
        return [("kns",), ("qns",), ("us",)] if piece[1] == 0 else [("utail",)]
    if kind == "attend":
        b, m = piece[1:]
        out = []
        if m + 1 < BT * NH:
            out.append(("s", b, m + 1))
        if 0 <= m < BT * NH:
            out.append(("pT", b, m))
        if m >= 1 and (m - 1) % NH == NH - 1:
            out.append(("yT", b, (m - 1) // NH))
        return out
    if kind == "sample":
        return ([("qrep", n) for n in range(B)] + [("ssT",), ("spT",)] + [("so", n) for n in range(B)])
    return []


def all_pieces():
    return [piece for l in range(L) for b in range(2) for piece, _ in pieces(l, b)]


def chunk_list():
    return [piece for piece in all_pieces() if piece[0] in ("p", "v", "wo", "q")]


def psum_jobs():
    names = [job for piece in all_pieces() for job in jobs_of(piece)]
    return {name: (i % NB, i // NB) for i, name in enumerate(names)}


def build(nc, x_prompt, x_sample, state_conv, state_win_k, state_win_v, state_pool, norm_mix, w_in_ab,
          conv_w, w_out_ab, pool_w, pool_b, pool_scale, norm_ffn, peer_wq, peer_subkeys, peer_u, peer_v,
          norm_final, y_prompt, y_sample, conv_prompt, conv_sample, win_k_prompt, win_k_sample,
          win_v_prompt, win_v_sample, pool_prompt, pool_sample):
    JOBS = psum_jobs()
    ctx = ExitStack()
    with ctx:
        def sb(name, shape, dt=f32):
            return ctx.enter_context(nc.sbuf_tensor(name, shape, dt))

        def sem(name):
            return ctx.enter_context(nc.semaphore(name))

        X = sb("X", [P, T + 1, D])
        H = sb("H", [P, (T + 1) * D])
        Hv = H[:, :].rearrange("p (s d) -> p s d", d=D)
        HT = sb("HT", [P, KD, HT_N])
        SC = sb("SC", [P, T * HC * NK + 2 * NK])
        RING = sb("RING", [P, (U_SLOTS + V_SLOTS) * D])
        WCH = sb("WCH", [P, NW, KD, WC])
        KT = sb("KT", [P, CA, SEQ])
        VN = sb("VN", [P, T, DA])
        YT = sb("YT", [P, KD, HT_N])
        SKT = sb("SKT", [P, HC, NK])
        G = sb("G", [P, D])
        hcur = sb("hcur", [P, D])
        hrep = sb("hrep", [P, D])
        ident = sb("ident", [P, P])
        COUNT = sb("COUNT", [P, T, P])
        MASKED = sb("MASKED", [P, T, P])
        POOL_CUR = sb("POOL_CUR", [P, NG, P])
        POOL_PREV = sb("POOL_PREV", [P, NG, P])
        POOL_FIRST = sb("POOL_FIRST", [P, NG, P])
        POOL_STATE_M = sb("POOL_STATE_M", [P, NG, B])
        POOL_NEW_M = sb("POOL_NEW_M", [P, NG, B])
        diag = sb("diag", [P, DIAGS, P])
        sel64 = sb("sel64", [P, B])
        ones = sb("ones", [P, 1])
        convw = sb("convw", [P, 3, CA])
        u_last = sb("u_last", [P, CA, 2])
        pT_s = sb("pT_s", [P, KD, B])
        ss = sb("ss", [P, T + 1])
        rstd = sb("rstd", [P, T + 1])
        negm = sb("negm", [P, 2])
        den = sb("den", [P, 2, NH])
        rden = sb("rden", [P, 2, NH])
        iota16 = sb("iota16", [P, TOP])
        W = sb("W", [P, 4 * 2 * NK])
        sc = W[:, 0:2 * NK].rearrange("p (c k) -> p c k", c=2)
        scw = W[:, 2 * NK:4 * NK].rearrange("p (c k) -> p c k", c=2)
        cand = W[:, 4 * NK:6 * NK]
        candw = W[:, 6 * NK:8 * NK]
        onehot = sb("onehot", [P, 2, TOP, TOP])
        sv = sb("sv", [P, 2, TOP])
        si = sb("si", [P, 2, TOP], u32)
        sif = sb("sif", [P, 2, TOP])
        ci = sb("ci", [P, TOP], u32)
        cij = sb("cij", [P, 2, TOP], u32)
        cijf = sb("cijf", [P, 2, TOP])
        picked = sb("picked", [P, 2, TOP])
        cs = sb("cs", [P, SETS, TOP])
        ncs = sb("ncs", [P, SETS])
        idx = sb("idx", [P, SETS, TOP], u32)
        ex = sb("ex", [P, SETS, TOP])
        exsum = sb("exsum", [P, SETS])
        rsum = sb("rsum", [P, 1])
        dots = sb("dots", [P, SETS, TOP])
        act_h = sb("act_h", [P, SETS, TOP])
        gate = sb("gate", [P, SETS, TOP])

        u_rows = RING[:, 0:U_SLOTS * D].rearrange("p (s d) -> p s d", d=D)
        v_rows = RING[:, U_SLOTS * D:].rearrange("p (s d) -> p s d", d=D)
        KV = 3 * DA
        kv = RING[:, 0:2 * KV].rearrange("p (a t n) -> p a t n", a=2, t=3)
        prod = RING[:, 2 * KV:3 * KV]
        masked = (RING[:, 3 * KV:3 * KV + DA], prod[:, 0:DA])
        o = 3 * KV + DA
        sk_nat0 = RING[:, o:o + HC * P].rearrange("p (h d) -> p h d", h=HC)
        o += HC * P
        q_s, k_s, v_s, unew = (RING[:, o + n * DA:o + (n + 1) * DA] for n in range(4))
        o += 4 * DA
        conv_rows = RING[0:3 * CA, o:o + P]
        conv_st_rows = RING[0:2 * B, o + P:o + P + DA]
        o += P + DA
        c_s, u_s, qT_s, kT_s = (RING[:, o + n * CA * B:o + (n + 1) * CA * B].rearrange("p (c b) -> p c b", c=CA)
                                for n in range(4))
        o += 4 * CA * B
        conv_st = RING[:, o:o + 2 * CA * B].rearrange("p (c b j) -> p c b j", c=CA, b=B)
        UW = BN + 2
        o = BT * HC * NK
        uT = SC[:, o:o + CA * UW].rearrange("p (c n) -> p c n", c=CA)
        o += CA * UW
        qT = SC[:, o:o + CA * BN].rearrange("p (c n) -> p c n", c=CA)
        o += CA * BN
        Y = SC[:, o:o + 2 * DA].rearrange("p (a n) -> p a n", a=2)
        S = H[:, 3 * D:4 * D].rearrange("p (a n) -> p a n", a=2)
        PT = H[:, 4 * D:5 * D].rearrange("p (a n) -> p a n", a=2)
        utail = S[:, 0, :]
        YTf = YT[:, :, :].rearrange("p k n -> p (k n)")
        qp = YTf[:, 0:2 * HT_N].rearrange("p (a n) -> p a n", a=2)
        sc_s = YTf[:, 2 * HT_N:2 * HT_N + 4 * NK].rearrange("p (a c k) -> p a c k", a=2, c=2)
        pT = [SC[:, b * BT * HC * NK:b * BT * HC * NK + BT * D].rearrange("p (t c n) -> p t c n", t=BT, c=KD)
              for b in range(2)]
        prev_rows = YTf[:, 2 * HT_N + 4 * NK:2 * HT_N + 4 * NK + D]
        poolw = KT[:, :, :].rearrange("p c n -> p (c n)").rearrange("p (g k n) -> p g k n", g=NG, k=2)
        pscale = VN[:, 0:2, :].rearrange("p a n -> p (a n)")
        pbias = VN[:, 2:4, :].rearrange("p a n -> p (a n)")
        HTf = HT[:, :, :].rearrange("p k n -> p (k n)")
        sk_nat1 = HTf[:, 0:HC * P].rearrange("p (h d) -> p h d", h=HC)
        pstate = HTf[:, 0:D]
        SCt = SC[:, 0:T * HC * NK].rearrange("p (t h k) -> p t h k", t=T, h=HC)
        sc64 = SC[:, T * HC * NK:T * HC * NK + 2 * NK]
        sel = W[:, :].rearrange("p (b n) -> p b n", b=B)
        dist = COUNT[:, :, :].bitcast(i32)
        tplus1 = cand[:, 0:P]
        window = cand[:, P:2 * P]
        POOL_STEPS = 8 + 5 * NG
        S_all = Y[:, 0, 0:3 * B * NH].rearrange("p (t b h) -> p t b h", t=3, b=B)
        SP_ = Y[:, 1, 0:2 * P + SAMPLE_ROWS]
        SPT = S[:, 0, 0:3 * B * NH].rearrange("p (t n) -> p t n", t=3)
        CHUNKS = chunk_list()

        PSUM = ctx.enter_context(nc.psum_tensor("PSUM", [P, 8, 512], f32))

        bank_full = [sem(f"bank_full{b}") for b in range(NB)]
        bank_emptied = [sem(f"bank_emptied{b}") for b in range(NB)]
        x_loaded = sem("x_loaded")
        x2_loaded = sem("x2_loaded")
        g_loaded = sem("g_loaded")
        small_loaded = sem("small_loaded")
        sk_loaded = sem("sk_loaded")
        w_loaded = [sem(f"w_loaded{n}") for n in range(NW)]
        kv_loaded = [sem(f"kv_loaded{n}") for n in range(2)]
        pool_loaded = sem("pool_loaded")
        sample_moved = [sem(f"sample_moved{n}") for n in range(2)]
        hrep_moved = sem("hrep_moved")
        own_stored = sem("own_stored")
        tail_stored = sem("tail_stored")
        state_loaded = sem("state_loaded")
        stored = sem("stored")
        pool_stored = sem("pool_stored")
        kstage_stored = [sem(f"kstage_stored{n}") for n in range(2)]
        cache_copied = [sem(f"cache_copied{n}") for n in range(2)]
        pool_consts = sem("pool_consts")
        consts = sem("consts")
        dve_chain = sem("dve_chain")
        dve_loop = sem("dve_loop")
        squares_ready = sem("squares_ready")
        root_ready = sem("root_ready")
        rows_normed = sem("rows_normed")
        kv_cleared = sem("kv_cleared")
        max_ready = sem("max_ready")
        exp_ready = sem("exp_ready")
        probs_ready = sem("probs_ready")
        y_done = sem("y_done")
        y_normed = sem("y_normed")
        k_scored = sem("k_scored")
        sy_done = sem("sy_done")
        sy_moved = sem("sy_moved")
        sprobs_ready = sem("sprobs_ready")
        smax_ready = sem("smax_ready")
        sexp_ready = sem("sexp_ready")
        u_landed = [sem(f"u_landed{s}") for s in range(U_SLOTS)]
        v_landed = [sem(f"v_landed{s}") for s in range(V_SLOTS)]
        prev_saved = sem("prev_saved")
        u_freed = sem("u_freed")
        v_freed = sem("v_freed")
        idx_ready = sem("idx_ready")
        cs_ready = sem("cs_ready")
        gates_exp = sem("gates_exp")
        gelu_done = sem("gelu_done")
        gate_ready = sem("gate_ready")
        diag_ready = sem("diag_ready")
        acc_added = sem("acc_added")
        passed = sem("passed")

        def bank(name):
            return PSUM[:, JOBS[name][0], :]

        def wait_full(eng, name):
            b, use = JOBS[name]
            eng.wait_ge(bank_full[b], use + 1)

        def emptied(ins, name):
            ins.then_inc(bank_emptied[JOBS[name][0]], 1)

        def wait_emptied(eng, name):
            b, use = JOBS[name]
            eng.wait_ge(bank_emptied[b], use + 1)

        def task(l, i, h):
            return l * TASKS + i * PH + h

        def sample_task(l):
            return l * TASKS + T * PH

        def unit(l, n):
            return l * (T + 1) + n

        def rows_by(e, n=None):
            return sum(len(slots) for slots in NORMS[:e]) + (len(NORMS[e]) if n is None else n)

        def wait_chunk(eng, piece):
            n = CHUNKS.index(piece)
            eng.wait_ge(w_loaded[n % NW], 16 * (n // NW + 1))
            return WCH[:, n % NW, :, :]

        block = ctx.enter_context(nc.Block())

        @block.sync
        def _(sp):
            stores = [0]
            w_in = w_in_ab[0].rearrange("(k p) n -> p k n", p=P)
            w_o = w_out_ab[0].rearrange("(k p) n -> p k n", p=P)

            def store(out, src):
                stores[0] += 16
                sp.dma_start(out, src).then_inc(stored, 16)

            def load_chunk(n):
                piece = CHUNKS[n]
                if piece[0] == "p":
                    src, c = w_in, "bcxqk".index(piece[2]) * CA + piece[3]
                elif piece[0] == "v":
                    src, c = w_in, 5 * CA + piece[2]
                elif piece[0] == "wo":
                    src, c = w_o, piece[2]
                else:
                    src, c = peer_wq[piece[1]].rearrange("(k p) n -> p k n", p=P), piece[3]
                sp.dma_start(WCH[:, n % NW, :, :], src[:, :, c * WC:(c + 1) * WC]).then_inc(w_loaded[n % NW], 16)

            def load_norm(e):
                if e:
                    sp.wait_ge(rows_normed, rows_by(e - 1))
                src = norm_final.unsqueeze(0) if e >= 8 else (norm_ffn if e % 2 else norm_mix)[e // 4:e // 4 + 1, :]
                sp.dma_start(G[:], src.to_broadcast([P, D])).then_inc(g_loaded, 16)

            def sample_attention():
                sp.wait_ge(kv_cleared, 1)
                for n in range(2 * B):
                    b, a = n % B, n % 2
                    cache, own = (state_win_k, k_s) if n < B else (state_win_v, v_s)
                    if n >= 2:
                        if n - 2 < B:
                            sp.wait_ge(k_scored, n - 1)
                        else:
                            wait_full(sp, ("so", n - 2 - B))
                    sp.dma_start(kv[:, a, 0, :], cache[0, b, PAST - P:PAST, :]).then_inc(kv_loaded[a], 16)
                    sp.dma_start(kv[:, a, 1, :], cache[0, b, PAST - 4 * P:PAST, :].rearrange("(r s) n -> r s n", s=4)[:, 0, :]).then_inc(kv_loaded[a], 16)
                    sp.dma_start(kv[0:64, a, 2, :], cache[0, b, :, :].rearrange("(r s) n -> r s n", s=16)[:, 0, :]).then_inc(kv_loaded[a], 16)
                    sp.dma_start(kv[64:65, a, 2, :], own[b:b + 1, :]).then_inc(kv_loaded[a], 16)

            def front(piece):
                kind = piece[0]
                if piece in CHUNKS and CHUNKS.index(piece) + NW < len(CHUNKS):
                    wait_full(sp, piece)
                    load_chunk(CHUNKS.index(piece) + NW)
                if kind == "normed":
                    load_norm(piece[1] + 1)
                if kind == "v" and piece[2] == CA - 1:
                    for c in range(CA):
                        wait_emptied(sp, ("v", piece[1], c))
                    for t in range(BT * piece[1], BT * piece[1] + BT):
                        store(win_v_prompt[0, t * P:(t + 1) * P, :], VN[:, t, :])
                if kind == "kn":
                    t = piece[1] * BT + piece[2]
                    wait_emptied(sp, piece)
                    sp.dma_start(win_k_prompt[0, t * P:(t + 1) * P, :], Y[:, t % 2, :]).then_inc(kstage_stored[t % 2], 16)
                if piece == ("tails", 0):
                    wait_emptied(sp, ("kns",))
                    wait_emptied(sp, ("us",))
                    for out, src in ((win_k_sample[0, :, PAST - 1, :], k_s), (win_v_sample[0, :, PAST - 1, :], v_s),
                                     (conv_sample[0, :, 1, :], unew)):
                        sp.dma_start(out, src[0:B, :]).then_inc(own_stored, 16)
                if piece == ("tails", 1):
                    wait_emptied(sp, ("utail",))
                    sp.dma_start(conv_prompt[0, 0, :, :], utail[0:2, :]).then_inc(tail_stored, 16)
                if kind == "sample":
                    sample_attention()
                if kind == "sc" and has_sample(*piece[1:3]) and piece[3] % 2 == 1:
                    h = piece[3] // 2
                    wait_emptied(sp, piece)
                    sp.dma_start(sc64[h * B:(h + 1) * B, :], sc_s[0:B, h % 2, :, :].rearrange("p c k -> p (c k)")).then_inc(sample_moved[h % 2], 16)
                if kind == "scored" and has_sample(*piece[1:3]):
                    for h in range(PH):
                        sp.dma_start(hrep[h * B:(h + 1) * B, :], Hv[0:B, 0, :]).then_inc(hrep_moved, 16)
                if piece == ("squares", 4):
                    wait_emptied(sp, ("yT", 1, BT - 1))
                    wait_full(sp, ("q", 0, 1, HC - 1))
                    sp.wait_ge(stored, stores[0])
                    sp.dma_start(sk_nat1, peer_subkeys[1].rearrange("h c k d -> k (h c) d")).then_inc(sk_loaded, 16)
                    sp.dma_start(poolw, pool_w[0].rearrange("g (k p) n -> p g k n", p=P)).then_inc(pool_loaded, 16)
                    sp.dma_start(pscale, pool_scale[0:1, :].to_broadcast([P, D])).then_inc(pool_loaded, 16)
                    sp.dma_start(pbias, pool_b.rearrange("o g n -> o (g n)").to_broadcast([P, D])).then_inc(pool_loaded, 16)
                if piece == ("squares", 6):
                    wait_full(sp, ("q", 1, 0, HC - 1))
                    sp.dma_start(pstate[0:B * PS, :], state_pool[0].rearrange("b j n -> (b j) n")).then_inc(state_loaded, 16)
                if piece == ("normed", 6):
                    sp.dma_start(pool_prompt[0, 0, :, :], Hv[P - PS:P, T, :]).then_inc(pool_stored, 16)
                    sp.dma_start(pool_sample[0, :, PS - 1, :], Hv[0:B, 0, :]).then_inc(pool_stored, 16)

            for t in range(BT):
                sp.dma_start(X[:, t + 1, :], x_prompt[0, t * P:(t + 1) * P, :]).then_inc(x_loaded, 16)
            sp.wait_ge(consts, 1)
            sp.dma_start(X[0:B, 0, :], x_sample.rearrange("b s d -> (b s) d")).then_inc(x_loaded, 16)
            load_norm(0)
            for n in range(NW):
                load_chunk(n)
            sp.dma_start(conv_rows, conv_w[0].rearrange("i (c p) -> (i c) p", p=P)).then_inc(small_loaded, 16)
            sp.dma_start(conv_st_rows, state_conv[0].rearrange("b j n -> (b j) n")).then_inc(small_loaded, 16)
            sp.dma_start(sk_nat0, peer_subkeys[0].rearrange("h c k d -> k (h c) d")).then_inc(sk_loaded, 16)
            for t in range(BT, T):
                sp.dma_start(X[:, t + 1, :], x_prompt[0, t * P:(t + 1) * P, :]).then_inc(x2_loaded, 16)
            store(conv_sample[0, :, 0, :], state_conv[0, :, 1, :])
            store(pool_sample[0, :, 0:PS - 1, :], state_pool[0, :, 1:PS, :])
            for piece in all_pieces():
                front(piece)
            for n, s in enumerate(NORMS[8]):
                sp.wait_ge(rows_normed, rows_by(8, n + 1))
                store(y_prompt[0, (s - 1) * P:s * P, :], Hv[:, s, :])
            load_norm(9)
            sp.wait_ge(rows_normed, rows_by(9))
            store(y_sample.rearrange("b s d -> (b s) d"), Hv[0:B, 0, :])
            sp.wait_ge(stored, stores[0])
            sp.wait_ge(pool_stored, 32)
            sp.wait_ge(own_stored, 48)
            sp.wait_ge(tail_stored, 16)
            for n in range(2):
                sp.wait_ge(kstage_stored[n], 16 * T // 2)
                sp.wait_ge(cache_copied[n], 16 * B)

        @block.gpsimd
        def _(pool):
            made = [0]

            def step(ins):
                made[0] += 1
                ins.then_inc(pool_consts, 1)
                pool.wait_ge(pool_consts, made[0])

            def keep(ap, base, cm, pattern, fill=0.0, op=ALU.is_ge):
                step(nc.gpsimd.affine_select(out=ap, in_=ap, compare_op=op, fill=fill, base=base,
                                             pattern=pattern, channel_multiplier=cm))

            step(nc.gpsimd.memset(ident[:], 0.0))
            keep(ident[:], 0, 1, [[-1, P]], fill=1.0, op=ALU.not_equal)
            step(nc.gpsimd.iota(dist, pattern=[[-P, T], [-1, P]], base=(T - 1) * P, channel_multiplier=1,
                                allow_small_or_imprecise_dtypes=True))
            step(nc.gpsimd.iota(iota16[:], pattern=[[1, TOP]], base=0, channel_multiplier=0,
                                allow_small_or_imprecise_dtypes=True))
            step(nc.gpsimd.iota(tplus1[:], pattern=[[1, P]], base=1, channel_multiplier=0,
                                allow_small_or_imprecise_dtypes=True))
            step(nc.gpsimd.memset(POOL_CUR[:], 1.0))
            step(nc.gpsimd.memset(POOL_PREV[:], 1.0))
            step(nc.gpsimd.memset(POOL_STATE_M[:], 1.0))
            n = 0
            for src, out in ((state_win_k, win_k_sample), (state_win_v, win_v_sample)):
                for b in range(B):
                    if n >= 2:
                        pool.wait_ge(cache_copied[n % 2], 16 * (n // 2))
                    pool.dma_start(out[0, b, 0:PAST - 1, :].rearrange("r n -> (r n)").rearrange("(a n) -> a n", a=P),
                                   src[0, b, 1:PAST, :].rearrange("r n -> (r n)").rearrange("(a n) -> a n", a=P)
                                   ).then_inc(cache_copied[n % 2], 16)
                    n += 1
                    if n % 2 == 0 and n <= 2 * NG:
                        g = n // 2 - 1
                        w = POOL_W[g]
                        keep(POOL_CUR[:, g, :], 0, -1, [[1, P]])
                        keep(POOL_CUR[:, g, :], w - 1, 1, [[-1, P]])
                        keep(POOL_PREV[:, g, :], w - 1 - P, 1, [[-1, P]])
                        keep(POOL_STATE_M[:, g, :], -(PS + 1 - w), 1, [[-PS, B]])
                        keep(POOL_STATE_M[:, g, :], PS - 1, -1, [[PS, B]])

            def gather(rows, slots, table, landed, st, n, k):
                pool.indirect_dma_start(
                    rows[0:n, k % slots, :], None, table.rearrange("l e d -> (l e) d"),
                    bass.IndirectOffsetOnAxis(ap=idx[0:n, st, k:k + 1], axis=0),
                ).then_inc(landed[k % slots], 16)

            def wait_for(semaphore, count):
                pool.wait_ge(semaphore, count)
                pool.sem_inc(passed, 1)

            def gather_u(st, tau, k):
                wait_for(u_freed, tau * TOP + k + 1)
                gather(u_rows, U_SLOTS, peer_u, u_landed, st, P, k)

            def gather_v(st, tau, n, k):
                if k % 2 == 0:
                    wait_for(v_freed, tau * TOP + k + 2)
                gather(v_rows, V_SLOTS, peer_v, v_landed, st, n, k)

            def gathers(tau, st, n):
                wait_for(idx_ready, tau + 2)
                for k in range(TOP):
                    gather_u((st + 1) % SETS, tau + 1, k)
                    gather_v(st, tau, n, k)

            wait_for(idx_ready, 1)
            for k in range(TOP):
                gather_u(0, 0, k)
            for l in range(L):
                with pool.Fori(0, T) as i:
                    for h in range(PH):
                        gathers(i * PH + task(l, 0, h), task(l, 0, h) % SETS, P)
                if l == 0:
                    gathers(sample_task(0), sample_task(0) % SETS, PH * B)
            for k in range(TOP):
                gather_v(sample_task(1) % SETS, sample_task(1), PH * B, k)

        @block.tensor
        def _(pe):
            opened = []

            def open_bank(name):
                b, use = JOBS[name]
                assert len(opened) == use * NB + b, name
                opened.append(name)
                if use:
                    pe.wait_ge(bank_emptied[b], use)
                return PSUM[:, b, :]

            def close_bank(ins, name):
                ins.then_inc(bank_full[JOBS[name][0]], 1)

            def transposes(name, width, pieces):
                out = open_bank(name)
                for n, src in enumerate(pieces):
                    rows, cols = src.shape
                    last = nc.tensor.transpose(out[0:cols, n * width:n * width + rows], src, ident[0:rows, 0:rows])
                close_bank(last, name)

            def chunks(row, n=4):
                return [row[:, c * P:(c + 1) * P] for c in range(n)]

            def wait_rows(l, b, e):
                for j in range(BT):
                    for half in range(2):
                        wait_emptied(pe, ("hT", e, j, half))
                if has_sample(l, b):
                    wait_emptied(pe, ("hT", e, "s", 0))

            def across(piece, width):
                w = wait_chunk(pe, piece)
                out = open_bank(piece)
                for k in range(KD):
                    last = nc.tensor.matmul(out[:, 0:width], w[:, k, :], HT[:, k, 0:width],
                                            start=(k == 0), stop=(k == KD - 1))
                close_bank(last, piece)

            def along(piece, rows, tiles, sample):
                w = wait_chunk(pe, piece)
                out = open_bank(piece)
                for j in range(tiles + sample):
                    m = P if j < tiles else B
                    for k in range(KD):
                        last = nc.tensor.matmul(out[0:m, j * P:(j + 1) * P], rows[:, k, j * P:j * P + m], w[:, k, :],
                                                start=(k == 0), stop=(k == KD - 1))
                close_bank(last, piece)

            def scores(b, m):
                j, h = divmod(m, NH)
                t = b * BT + j
                lo = HD * (h % 2)
                out = open_bank(("s", b, m))
                close_bank(nc.tensor.matmul(out[:, 0:(t + 1) * P], qT[lo:lo + HD, h // 2, j * P:(j + 1) * P],
                                            KT[lo:lo + HD, h // 2, 0:(t + 1) * P], start=True, stop=True), ("s", b, m))

            def weighted(b, m):
                j, h = divmod(m, NH)
                t = b * BT + j
                wait_emptied(pe, ("pT", b, m))
                if h == 0 and t >= 1:
                    pe.wait_ge(y_normed, t)
                for kt in range(t + 1):
                    last = nc.tensor.matmul(PSUM[:, 5, h * HD:(h + 1) * HD], PT[:, m % 2, kt * P:(kt + 1) * P],
                                            VN[:, kt, h * HD:(h + 1) * HD], start=(kt == 0), stop=(kt == t))
                last.then_inc(y_done, 1)
                if h == NH - 1:
                    pe.wait_ge(y_normed, t + 1)
                    transposes(("yT", b, j), P, chunks(Y[:, t % 2, :]))

            def attend(b, m):
                if m + 1 < BT * NH:
                    scores(b, m + 1)
                if 0 <= m < BT * NH:
                    pe.wait_ge(probs_ready, b * BT * NH + m + 1)
                    transposes(("pT", b, m), P, chunks(S[:, m % 2, :], b * BT + m // NH + 1))
                if m >= 1:
                    weighted(b, m - 1)

            def gather_heads(b):
                wait_emptied(pe, ("so", b))
                for c in range(CA):
                    last = nc.tensor.matmul(PSUM[:, 6, c * B + b:c * B + b + 1],
                                            masked[b % 2][0:NH, c * P:(c + 1) * P], ones[0:NH, :], start=True, stop=True)
                last.then_inc(sy_done, 1)

            def sample_attention():
                wait_emptied(pe, ("qns",))
                pe.wait_ge(consts, 3)
                for b in range(B):
                    out = open_bank(("qrep", b))
                    close_bank(nc.tensor.matmul(out[:, :], sel[0:B, b, :], q_s[0:B, :], start=True, stop=True), ("qrep", b))
                pe.wait_ge(k_scored, B)
                out = open_bank(("ssT",))
                for c in range(3):
                    last = nc.tensor.transpose(out[0:B * NH, c * P:(c + 1) * P],
                                               S_all[:, c, :, :].rearrange("p b h -> p (b h)"), ident[:])
                close_bank(last, ("ssT",))
                pe.wait_ge(sprobs_ready, 1)
                out = open_bank(("spT",))
                for c in range(3):
                    last = nc.tensor.transpose(out[0:LOC[c], c * B * NH:(c + 1) * B * NH],
                                               SP_[0:B * NH, c * P:c * P + LOC[c]], ident[0:B * NH, 0:B * NH])
                close_bank(last, ("spT",))
                wait_emptied(pe, ("spT",))
                for b in range(B):
                    pe.wait_ge(kv_loaded[b % 2], 64 * (B // 2 + b // 2 + 1))
                    out = open_bank(("so", b))
                    for c in range(3):
                        last = nc.tensor.matmul(out[0:NH, :], SPT[0:LOC[c], c, b * NH:(b + 1) * NH],
                                                kv[0:LOC[c], b % 2, c, :], start=(c == 0), stop=(c == 2))
                    close_bank(last, ("so", b))
                    if b:
                        gather_heads(b - 1)
                gather_heads(B - 1)

            def pooled(b, j, half):
                t = b * BT + j
                out = open_bank(("pp", b, j, half))
                before = prev_rows if (b, j) == (1, 0) else Hv[:, t, :]
                for c in range(4):
                    ch = 4 * half + c
                    g = ch * P // GW
                    cols = slice(ch * P, (ch + 1) * P)
                    o_ = out[:, c * P:(c + 1) * P]
                    last = nc.tensor.matmul(o_, Hv[:, t + 1, cols], (POOL_CUR if t else POOL_FIRST)[:, g, :],
                                            start=True, stop=(t == 0))
                    if t:
                        if (b, j) == (1, 0):
                            pe.wait_ge(prev_saved, 1)
                        last = nc.tensor.matmul(o_, before[:, cols], POOL_PREV[:, g, :], start=False, stop=True)
                close_bank(last, ("pp", b, j, half))

            def pooled_sample():
                pe.wait_ge(state_loaded, 16)
                out = open_bank(("pps",))
                for ch in range(KD):
                    g = ch * P // GW
                    o_ = out[:, ch * B:(ch + 1) * B]
                    nc.tensor.matmul(o_, pstate[0:B * PS, ch * P:(ch + 1) * P], POOL_STATE_M[0:B * PS, g, :],
                                     start=True, stop=False)
                    last = nc.tensor.matmul(o_, Hv[0:B, 0, ch * P:(ch + 1) * P], POOL_NEW_M[0:B, g, :],
                                            start=False, stop=True)
                close_bank(last, ("pps",))

            def pool_mapped(b, j, half):
                pe.wait_ge(pool_loaded, 48)
                if j < BT:
                    wait_emptied(pe, ("pp", b, j, half))
                else:
                    wait_emptied(pe, ("pps",))
                src, m = (pT[b][:, j, :, :], P) if j < BT else (pT_s, B)
                out = open_bank(("pl", b, j, half))
                for n in range(2):
                    for k in range(2):
                        g = 2 * half + n
                        last = nc.tensor.matmul(out[0:m, n * GW:(n + 1) * GW], src[:, 2 * g + k, :],
                                                poolw[:, g, k, :], start=(k == 0), stop=(k == 1))
                close_bank(last, ("pl", b, j, half))

            def front(piece):
                kind = piece[0]
                if kind == "hT":
                    e, j, half = piece[1:]
                    if j == "s":
                        pe.wait_ge(rows_normed, rows_by(e))
                        transposes(piece, B, chunks(Hv[0:B, 0, :], KD))
                    else:
                        pe.wait_ge(rows_normed, rows_by(e, j + 1))
                        slot = NORMS[e][j]
                        transposes(piece, P, chunks(Hv[:, slot, half * 512:(half + 1) * 512]))
                if kind == "small":
                    pe.wait_ge(small_loaded, 32)
                    transposes(("conv_state",), 2 * B, chunks(conv_st_rows))
                    transposes(("conv_w",), 3 * CA, [conv_rows])
                if kind == "p":
                    b = piece[1]
                    if piece[2:] == ("c", 0):
                        wait_rows(0, b, 2 * b)
                    across(piece, HT_N if b == 0 else BN)
                if kind == "v":
                    along(piece, HT, BT, piece[1] == 0)
                if kind == "kn":
                    b, j = piece[1:]
                    for c in range(CA):
                        wait_emptied(pe, ("p", b, "k", c))
                    transposes(piece, P, [KT[:, c, (b * BT + j) * P:(b * BT + j + 1) * P] for c in range(CA)])
                if kind == "tails":
                    b = piece[1]
                    for kind_ in "xq":
                        for c in range(CA):
                            wait_emptied(pe, ("p", b, kind_, c))
                    if b == 0:
                        transposes(("kns",), P, [kT_s[:, c, :] for c in range(CA)])
                        transposes(("qns",), P, [qT_s[:, c, :] for c in range(CA)])
                        transposes(("us",), P, [u_s[:, c, :] for c in range(CA)])
                    else:
                        transposes(("utail",), P, [uT[:, c, BN:BN + 2] for c in range(CA)])
                if kind == "attend":
                    b, m = piece[1:]
                    if m == -1:
                        for c in range(CA):
                            wait_emptied(pe, ("v", b, c))
                    attend(b, m)
                if kind == "sample":
                    sample_attention()
                if kind == "wo":
                    b, c = piece[1:]
                    if c == 0:
                        for n in range(CA):
                            wait_emptied(pe, ("p", b, "b", n))
                        for j in range(BT):
                            wait_emptied(pe, ("yT", b, j))
                        if b == 0:
                            pe.wait_ge(sy_moved, 1)
                    along(piece, YT, BT, b == 0)
                if kind == "skT":
                    l, j = piece[1:]
                    pe.wait_ge(sk_loaded, 16 * (l + 1))
                    nat = (sk_nat0, sk_nat1)[l]
                    transposes(piece, P, [nat[:, 4 * j + c, :] for c in range(4)])
                if kind == "pp":
                    b, j, half = piece[1:]
                    pe.wait_ge(rows_normed, rows_by(4 + 2 * b, j + 1))
                    pooled(b, j, half)
                if kind == "pps":
                    pe.wait_ge(rows_normed, rows_by(6))
                    pooled_sample()
                if kind == "pl":
                    pool_mapped(*piece[1:])
                if kind == "q":
                    l, b, hc = piece[1:]
                    if hc == 0:
                        wait_rows(l, b, 4 * l + 2 * b + 1)
                        for j in range(4):
                            wait_emptied(pe, ("skT", l, j))
                    across(piece, HT_N if has_sample(l, b) else BN)
                if kind == "sc":
                    l, b, hc = piece[1:]
                    wait_emptied(pe, ("q", l, b, hc))
                    out = open_bank(piece)
                    for j in range(BT + has_sample(l, b)):
                        m = P if j < BT else B
                        last = nc.tensor.matmul(out[0:m, j * P:(j + 1) * P], qp[:, hc % 2, j * P:j * P + m],
                                                SKT[:, hc, :], start=True, stop=True)
                    close_bank(last, piece)

            def accumulate(k, tau, n, out_n, first, last_one):
                pe.wait_ge(v_landed[k % V_SLOTS], tau * (16 * TOP // V_SLOTS) + 16 * (k // V_SLOTS + 1))
                pe.wait_ge(diag_ready, tau * TOP + k + 1)
                for half in range(2):
                    last = nc.tensor.matmul(PSUM[0:out_n, 6 + half, :], diag[0:n, k % DIAGS, 0:out_n],
                                            v_rows[0:n, k % V_SLOTS, half * 512:(half + 1) * 512],
                                            start=first and k == 0, stop=last_one and k == TOP - 1,
                                            skip_group_check=True)
                last.then_inc(v_freed, 1)

            def tile_unit(l, i, between):
                if not between or unit(l, i):
                    pe.wait_ge(acc_added, i + unit(l, 0))
                for h in range(PH):
                    for k in range(TOP):
                        accumulate(k, i * PH + task(l, 0, h), P, P, h == 0, h == PH - 1)
                        if between:
                            for piece in AGENDA.get(task(l, i, h) * TOP + k, ()):
                                front(piece)

            pe.wait_ge(consts, 2)
            for piece, _ in pieces(0, 0):
                front(piece)
            pe.sem_inc(v_freed, V_SLOTS)
            for l in range(L):
                looped = 0 if l == 0 else BT
                for i in range(T - looped):
                    tile_unit(l, i, True)
                if looped:
                    with pe.Fori(T - looped, T) as i:
                        tile_unit(l, i, False)
                pe.wait_ge(acc_added, unit(l, T))
                for k in range(TOP):
                    accumulate(k, sample_task(l), PH * B, B, True, True)
            assert len(opened) == len(JOBS)

        @block.scalar
        def _(act):
            def copy_out(name, out, src, scale=1.0):
                wait_full(act, name)
                emptied(nc.scalar.activation(out, src, ACT.Copy, scale=scale), name)

            def wide(name, n=4, width=P):
                return bank(name)[:, 0:n * width].rearrange("p (c n) -> p c n", c=n)

            def two_tiles(piece, n=P):
                return bank(piece)[:, 0:BT * n].rearrange("p (t n) -> p t n", t=BT)

            def attend(b, m):
                n = BT * NH
                if 0 <= m < n:
                    w = (b * BT + m // NH + 1) * P
                    act.wait_ge(max_ready, b * n + m + 1)
                    nc.scalar.activation(S[:, m % 2, 0:w], S[:, m % 2, 0:w], ACT.Exp,
                                         bias=negm[:, m % 2:m % 2 + 1]).then_inc(exp_ready, 1)
                if m >= 1:
                    w = (b * BT + (m - 1) // NH + 1) * P
                    if m >= 3:
                        act.wait_ge(y_done, b * n + m - 2)
                    copy_out(("pT", b, m - 1), PT[:, (m - 1) % 2, 0:w], bank(("pT", b, m - 1))[:, 0:w])
                if (m >= 2 and (m - 2) % NH == NH - 1) or m == n:
                    j = (m - 2) // NH
                    copy_out(("yT", b, j), YT[:, CA:2 * CA, j * P:(j + 1) * P], wide(("yT", b, j)))

            def front(piece):
                kind = piece[0]
                if kind == "squares":
                    act.wait_ge(squares_ready, piece[1] + 1)
                    nc.scalar.activation(rstd[:], ss[:], ACT.Sqrt).then_inc(root_ready, 1)
                if kind == "hT":
                    e, j, half = piece[1:]
                    if j == "s":
                        copy_out(piece, HT[:, :, BN:HT_N], wide(piece, KD, B))
                    else:
                        copy_out(piece, HT[:, 4 * half:4 * half + 4, j * P:(j + 1) * P], wide(piece))
                if kind == "skT":
                    copy_out(piece, SKT[:, 4 * piece[2]:4 * piece[2] + 4, :], wide(piece))
                if kind == "p" and piece[2] in "cqk":
                    b, k, c = piece[1:]
                    big, small, scale = {"c": (uT[:, c, 2:UW], c_s, 1.0), "q": (qT[:, c, :], qT_s, HD ** -0.5),
                                         "k": (KT[:, c, b * BN:(b + 1) * BN], kT_s, 1.0)}[k]
                    wait_full(act, piece)
                    last = nc.scalar.activation(big, bank(piece)[:, 0:BN], ACT.Copy, scale=scale)
                    if b == 0:
                        last = nc.scalar.activation(small[:, c, :], bank(piece)[:, BN:HT_N], ACT.Copy, scale=scale)
                    emptied(last, piece)
                if kind == "v":
                    b, c = piece[1:]
                    cols = slice(c * P, (c + 1) * P)
                    wait_full(act, piece)
                    last = nc.scalar.activation(VN[:, b * BT:(b + 1) * BT, cols], two_tiles(piece), ACT.Copy)
                    if b == 0:
                        last = nc.scalar.activation(v_s[0:B, cols], bank(piece)[0:B, BN:BN + P], ACT.Copy)
                    emptied(last, piece)
                if kind == "kn":
                    t = piece[1] * BT + piece[2]
                    copy_out(piece, Y[:, t % 2, :], bank(piece))
                if piece == ("tails", 0):
                    copy_out(("kns",), k_s[0:B, :], bank(("kns",))[0:B, :])
                    copy_out(("qns",), q_s[0:B, :], bank(("qns",))[0:B, :])
                    copy_out(("us",), unew[0:B, :], bank(("us",))[0:B, :])
                if piece == ("tails", 1):
                    copy_out(("utail",), utail[0:2, :], bank(("utail",))[0:2, :])
                if kind == "attend":
                    attend(*piece[1:])
                if kind == "sample":
                    act.wait_ge(smax_ready, 1)
                    nc.scalar.activation(SP_[0:B * NH, :], bank(("ssT",))[0:B * NH, 0:2 * P + SAMPLE_ROWS], ACT.Exp,
                                         bias=negm[0:B * NH, 0:1]).then_inc(sexp_ready, 1)
                if kind == "pp":
                    b, j, half = piece[1:]
                    copy_out(piece, pT[b][:, j, 4 * half:4 * half + 4, :], wide(piece))
                if kind == "pps":
                    copy_out(piece, pT_s[:, :, :], wide(piece, KD, B))
                if kind == "q":
                    l, b, hc = piece[1:]
                    if hc >= 2:
                        wait_full(act, ("sc", l, b, hc - 2))
                    w = HT_N if has_sample(l, b) else BN
                    copy_out(piece, qp[:, hc % 2, 0:w], bank(piece)[:, 0:w])

            def gates(par, tau):
                act.wait_ge(cs_ready, tau + 1)
                nc.scalar.activation(ex[:, par, :], cs[:, par, :], ACT.Exp, bias=ncs[:, par:par + 1],
                                     accum_out=exsum[:, par:par + 1]).then_inc(gates_exp, 1)

            def activate(st, tau, n):
                act.wait_ge(u_freed, tau * TOP + TOP + U_SLOTS)
                nc.scalar.activation(act_h[0:n, st, :], dots[0:n, st, :], ACT.Gelu).then_inc(gelu_done, 1)
                act.wait_ge(gate_ready, tau + 1)

            def diagonal(st, tau, n, selector, out_n, k):
                act.wait_ge(v_freed, tau * TOP + k + 1 + V_SLOTS - DIAGS)
                nc.scalar.activation(diag[0:n, k % DIAGS, 0:out_n], selector, ACT.Copy,
                                     scale=gate[0:n, st, k:k + 1]).then_inc(diag_ready, 1)

            def tile_unit(l, i, between):
                for h in range(PH):
                    now = task(l, 0, h)
                    gates((now + 1) % SETS, i * PH + now + 1)
                    activate(now % SETS, i * PH + now, P)
                    for k in range(TOP):
                        diagonal(now % SETS, i * PH + now, P, ident[:], P, k)
                        if between:
                            for piece in AGENDA.get(task(l, i, h) * TOP + k, ()):
                                front(piece)

            for piece, _ in pieces(0, 0):
                front(piece)
            gates(0, 0)
            for l in range(L):
                looped = 0 if l == 0 else BT
                for i in range(T - looped):
                    tile_unit(l, i, True)
                if looped:
                    with act.Fori(T - looped, T) as i:
                        tile_unit(l, i, False)
                tau = sample_task(l)
                if l == 0:
                    gates((tau + 1) % SETS, tau + 1)
                activate(tau % SETS, tau, PH * B)
                for k in range(TOP):
                    diagonal(tau % SETS, tau, PH * B, sel64[0:PH * B, :], B, k)
            front(("squares", 8))
            front(("squares", 9))

        @block.vector
        def _(dve):
            chain = {"sem": dve_chain, "n": 0}

            def step(ins):
                chain["n"] += 1
                ins.then_inc(chain["sem"], 1)
                dve.wait_ge(chain["sem"], chain["n"])

            def begin_loop():
                chain["static"] = chain["n"]
                chain["sem"], chain["n"] = dve_loop, 0

            def end_body():
                dve.sem_clear(dve_loop)
                chain["n"] = 0

            def end_loop():
                chain["sem"], chain["n"] = dve_chain, chain["static"]

            V = nc.vector

            def squares(e):
                for s in NORMS[e]:
                    n = P if s else B
                    chain["n"] += 1
                    V.tensor_tensor_reduce(out=Hv[0:n, s, :], in0=X[0:n, s, :], in1=X[0:n, s, :], scale=1.0,
                                           scalar=0.0, op0=ALU.mult, op1=ALU.add,
                                           accum_out=ss[0:n, s:s + 1]).then_inc(dve_chain, 1)
                dve.wait_ge(dve_chain, chain["n"])
                V.tensor_scalar(ss[:], ss[:], 1.0 / D, EPS, ALU.mult, ALU.add).then_inc(squares_ready, 1)

            def normed_rows(e):
                dve.wait_ge(root_ready, e + 1)
                step(V.reciprocal(rstd[:], rstd[:]))
                dve.wait_ge(g_loaded, 16 * (e + 1))
                for s in NORMS[e]:
                    n = P if s else B
                    V.scalar_tensor_tensor(out=Hv[0:n, s, :], in0=X[0:n, s, :], scalar=rstd[0:n, s:s + 1],
                                           in1=G[0:n, :], op0=ALU.mult, op1=ALU.mult).then_inc(rows_normed, 1)

            V.memset(X[:, 0, :], 0.0).then_inc(consts, 1)
            step(V.memset(ss[:], 1.0))
            step(V.memset(ones[:], 1.0))
            step(V.memset(sc64[:], 0.0))
            V.memset(RING[:, 0:2 * KV], 0.0).then_inc(kv_cleared, 1)
            dve.wait_ge(pool_consts, 8)
            t0 = S[:, 0, :].rearrange("p (a b) -> p a b", a=T)
            t1 = S[:, 1, :].rearrange("p (a b) -> p a b", a=T)
            t2 = PT[:, 0, :].rearrange("p (a b) -> p a b", a=T)
            ti = PT[:, 1, :].rearrange("p (a b) -> p a b", a=T).bitcast(i32)
            step(V.tensor_scalar(t0, dist, 128, None, ALU.is_le))
            for mask in (3, 15):
                step(V.tensor_scalar(ti, dist, mask, None, ALU.bitwise_and))
                step(V.tensor_scalar(t1, ti, 0, None, ALU.is_equal))
                step(V.tensor_tensor(t0, t0, t1, ALU.add))
            step(V.tensor_scalar(t2, dist, 0, None, ALU.is_ge))
            step(V.tensor_tensor(COUNT[:], t0, t2, ALU.mult))
            step(V.tensor_scalar(MASKED[:], COUNT[:], 0.0, NEG, ALU.is_equal, ALU.mult))
            step(V.tensor_reduce(sel64[0:PH * B, :], ident[0:PH * B, 0:PH * B].rearrange("p (h b) -> p b h", b=B),
                                 AX.X, ALU.add))
            step(V.memset(rden[:], 0.0))
            V.memset(den[:], 0.0).then_inc(consts, 1)
            dve.wait_ge(pool_consts, POOL_STEPS)
            for g, w in enumerate(POOL_W):
                step(V.tensor_scalar(window, tplus1, float(w), None, ALU.min))
                step(V.reciprocal(window, window))
                step(V.tensor_tensor(POOL_FIRST[:, g, :], POOL_CUR[:, g, :], window, ALU.mult))
                step(V.tensor_tensor(POOL_FIRST[:, g, :], POOL_FIRST[:, g, :], ident[:], ALU.subtract))
                step(V.tensor_scalar(POOL_CUR[:, g, :], POOL_CUR[:, g, :], 1.0 / w, None, ALU.mult))
                step(V.tensor_tensor(POOL_CUR[:, g, :], POOL_CUR[:, g, :], ident[:], ALU.subtract))
                step(V.tensor_scalar(POOL_PREV[:, g, :], POOL_PREV[:, g, :], 1.0 / w, None, ALU.mult))
                step(V.tensor_scalar(POOL_STATE_M[:, g, :], POOL_STATE_M[:, g, :], 1.0 / w, None, ALU.mult))
                step(V.tensor_scalar(POOL_NEW_M[:, g, :], ident[:, 0:B], 1.0 / w - 1.0, None, ALU.mult))
            step(V.tensor_copy(sel[0:B, :, :], ident[0:B, 0:B].unsqueeze(2).to_broadcast([B, B, P])))
            V.memset(negm[:], 0.0).then_inc(consts, 1)
            dve.wait_ge(consts, 3)

            def sample_placed(l):
                for n in range(2):
                    dve.wait_ge(sample_moved[n], 16 * PH // 2 * (l + 1))

            def conv_consts():
                wait_full(dve, ("conv_state",))
                emptied(V.tensor_copy(conv_st[:, :, :, :].rearrange("p c b j -> p (c b j)"),
                                      bank(("conv_state",))[:, 0:CA * 2 * B]), ("conv_state",))
                wait_full(dve, ("conv_w",))
                emptied(V.tensor_copy(convw[:, :, :].rearrange("p i c -> p (i c)"), bank(("conv_w",))[:, 0:3 * CA]),
                        ("conv_w",))
                wait_emptied(dve, ("conv_state",))
                wait_emptied(dve, ("conv_w",))

            def conv_input(b, c):
                piece = ("p", b, "x", c)
                if b == 0:
                    V.memset(uT[:, c, 0:2], 0.0)
                else:
                    V.tensor_copy(uT[:, c, 0:2], u_last[:, c, :])
                wait_emptied(dve, ("p", b, "c", c))
                wait_full(dve, piece)
                last = V.tensor_tensor(uT[:, c, 2:UW], bank(piece)[:, 0:BN], uT[:, c, 2:UW], ALU.mult)
                if b == 0:
                    last = V.tensor_tensor(u_s[:, c, :], bank(piece)[:, BN:HT_N], c_s[:, c, :], ALU.mult)
                emptied(last, piece)

            def convolved(b, c):
                piece = ("p", b, "b", c)
                if b == 1 and c == 0:
                    sample_placed(0)
                for n in range(CA):
                    wait_emptied(dve, ("p", b, "x", n))
                if b == 0 and c == 0:
                    step(V.tensor_copy(u_last[:], uT[:, :, BN:UW]))
                y, ys = YT[:, c, 0:BN], YT[:, c, BN:HT_N]
                step(V.tensor_scalar(y, uT[:, c, 0:BN], convw[:, 0, c:c + 1], None, ALU.mult))
                step(V.scalar_tensor_tensor(out=y, in0=uT[:, c, 1:BN + 1], scalar=convw[:, 1, c:c + 1], in1=y,
                                            op0=ALU.mult, op1=ALU.add))
                step(V.scalar_tensor_tensor(out=y, in0=uT[:, c, 2:UW], scalar=convw[:, 2, c:c + 1], in1=y,
                                            op0=ALU.mult, op1=ALU.add))
                if b == 0:
                    step(V.tensor_scalar(ys, conv_st[:, c, :, 0], convw[:, 0, c:c + 1], None, ALU.mult))
                    step(V.scalar_tensor_tensor(out=ys, in0=conv_st[:, c, :, 1], scalar=convw[:, 1, c:c + 1], in1=ys,
                                                op0=ALU.mult, op1=ALU.add))
                    step(V.scalar_tensor_tensor(out=ys, in0=u_s[:, c, :], scalar=convw[:, 2, c:c + 1], in1=ys,
                                                op0=ALU.mult, op1=ALU.add))
                wait_full(dve, piece)
                last = V.tensor_tensor(y, bank(piece)[:, 0:BN], y, ALU.mult)
                if b == 0:
                    last = V.tensor_tensor(ys, bank(piece)[:, BN:HT_N], ys, ALU.mult)
                emptied(last, piece)

            def masked_scores(b, m):
                t = b * BT + m // NH
                n = (t + 1) * P
                if m >= 2:
                    wait_full(dve, ("pT", b, m - 2))
                elif b == 1:
                    dve.wait_ge(tail_stored, 16)
                wait_full(dve, ("s", b, m))
                emptied(V.tensor_tensor(S[:, m % 2, 0:n], bank(("s", b, m))[:, 0:n],
                                        MASKED[:, T - 1 - t:T, :].rearrange("p a b -> p (a b)"), ALU.add), ("s", b, m))
                wait_emptied(dve, ("s", b, m))
                step(V.tensor_reduce(negm[:, m % 2:m % 2 + 1], S[:, m % 2, 0:n], AX.X, ALU.max))
                V.tensor_scalar(negm[:, m % 2:m % 2 + 1], negm[:, m % 2:m % 2 + 1], -1.0, None, ALU.mult).then_inc(max_ready, 1)

            def counted(b, m):
                j, h = divmod(m, NH)
                t = b * BT + j
                n = (t + 1) * P
                dve.wait_ge(exp_ready, b * BT * NH + m + 1)
                V.tensor_tensor_reduce(out=S[:, m % 2, 0:n], in0=S[:, m % 2, 0:n],
                                       in1=COUNT[:, T - 1 - t:T, :].rearrange("p a b -> p (a b)"), scale=1.0, scalar=0.0,
                                       op0=ALU.mult, op1=ALU.add, accum_out=den[:, t % 2, h:h + 1]).then_inc(probs_ready, 1)

            def attention_normed(t):
                dve.wait_ge(probs_ready, (t + 1) * NH)
                step(V.reciprocal(rden[:, t % 2, :], den[:, t % 2, :]))
                dve.wait_ge(y_done, (t + 1) * NH)
                dve.wait_ge(kstage_stored[t % 2], 16 * (t // 2 + 1))
                V.tensor_tensor(Y[:, t % 2, :].rearrange("p (h d) -> p h d", h=NH),
                                PSUM[:, 5, :].rearrange("p (h d) -> p h d", h=NH),
                                rden[:, t % 2, :].unsqueeze(2).to_broadcast([P, NH, HD]), ALU.mult).then_inc(y_normed, 1)

            def attend(b, m):
                if m + 1 < BT * NH:
                    masked_scores(b, m + 1)
                if 0 <= m < BT * NH:
                    counted(b, m)
                if m >= 1 and (m - 1) % NH == NH - 1:
                    attention_normed(b * BT + (m - 1) // NH)

            def sample_attention():
                for t in range(BT):
                    wait_full(dve, ("yT", 0, t))
                for b in range(B):
                    dve.wait_ge(kv_loaded[b % 2], 64 * (b // 2 + 1))
                    wait_full(dve, ("qrep", b))
                    if b:
                        dve.wait_ge(k_scored, b)
                    emptied(V.tensor_tensor(prod.rearrange("p (t n) -> p t n", t=3), kv[:, b % 2, :, :],
                                            bank(("qrep", b)).unsqueeze(1).to_broadcast([P, 3, DA]), ALU.mult), ("qrep", b))
                    wait_emptied(dve, ("qrep", b))
                    V.tensor_reduce(S_all[:, :, b, :], prod.rearrange("p (t h d) -> p t h d", t=3, h=NH), AX.X,
                                    ALU.add).then_inc(k_scored, 1)
                R = B * NH
                NS = 2 * P + SAMPLE_ROWS
                wait_full(dve, ("ssT",))
                step(V.tensor_reduce(negm[0:R, 0:1], bank(("ssT",))[0:R, 0:NS], AX.X, ALU.max))
                V.tensor_scalar(negm[0:R, 0:1], negm[0:R, 0:1], -1.0, None, ALU.mult).then_inc(smax_ready, 1)
                dve.wait_ge(sexp_ready, 1)
                emptied(V.tensor_scalar(SP_[0:R, NS - 1:NS], SP_[0:R, NS - 1:NS], 3.0, None, ALU.mult), ("ssT",))
                wait_emptied(dve, ("ssT",))
                step(V.tensor_reduce(den[0:R, 0, 0:1], SP_[0:R, 0:NS], AX.X, ALU.add))
                step(V.reciprocal(rden[0:R, 0, 0:1], den[0:R, 0, 0:1]))
                V.tensor_scalar(SP_[0:R, 0:NS], SP_[0:R, 0:NS], rden[0:R, 0, 0:1], None, ALU.mult).then_inc(sprobs_ready, 1)
                wait_full(dve, ("spT",))
                for c in range(3):
                    ins = V.tensor_copy(SPT[0:LOC[c], c, :], bank(("spT",))[0:LOC[c], c * R:(c + 1) * R])
                    if c < 2:
                        step(ins)
                emptied(ins, ("spT",))
                for b in range(B):
                    wait_full(dve, ("so", b))
                    if b >= 2:
                        dve.wait_ge(sy_done, b - 1)
                    emptied(V.tensor_tensor(masked[b % 2][0:NH, :].rearrange("p (h d) -> p h d", h=NH),
                                            bank(("so", b))[0:NH, :].rearrange("p (h d) -> p h d", h=NH),
                                            ident[0:NH, 0:NH].unsqueeze(2).to_broadcast([NH, NH, HD]), ALU.mult), ("so", b))
                dve.wait_ge(sy_done, B)
                V.tensor_copy(YT[:, CA:2 * CA, BN:HT_N],
                              PSUM[:, 6, 0:CA * B].rearrange("p (c b) -> p c b", c=CA)).then_inc(sy_moved, 1)

            def projected(b, c):
                piece = ("wo", b, c)
                cols = slice(c * P, (c + 1) * P)
                wait_full(dve, piece)
                rows = X[:, b * BT + 1:(b + 1) * BT + 1, cols]
                last = V.tensor_tensor(rows, bank(piece)[:, 0:BN].rearrange("p (t n) -> p t n", t=BT), rows, ALU.add)
                if b == 0:
                    last = V.tensor_tensor(X[0:B, 0, cols], bank(piece)[0:B, BN:BN + P], X[0:B, 0, cols], ALU.add)
                emptied(last, piece)
                if c == KD - 1:
                    for n in range(KD):
                        wait_emptied(dve, ("wo", b, n))

            def pool_added(b, j, half):
                piece = ("pl", b, j, half)
                s, n = (b * BT + j + 1, P) if j < BT else (0, B)
                cols = slice(half * 512, (half + 1) * 512)
                out = bank(piece)[0:n, :]
                wait_full(dve, piece)
                dve.wait_ge(pool_loaded, 48)
                step(V.tensor_tensor(out, out, pbias[0:n, cols], ALU.add))
                step(V.tensor_tensor(out, out, pscale[0:n, cols], ALU.mult))
                emptied(V.tensor_tensor(X[0:n, s, cols], out, X[0:n, s, cols], ALU.add), piece)
                wait_emptied(dve, piece)

            def key_scores(l, b, hc):
                piece = ("sc", l, b, hc)
                h = hc // 2
                wait_full(dve, piece)
                last = V.tensor_copy(SCt[:, b * BT:(b + 1) * BT, hc, :],
                                     bank(piece)[:, 0:BN].rearrange("p (t k) -> p t k", t=BT))
                if has_sample(l, b):
                    if h >= 2 or l:
                        dve.wait_ge(sample_moved[h % 2], 16 * (PH // 2 * l + h // 2))
                    last = V.tensor_copy(sc_s[0:B, h % 2, hc % 2, :], bank(piece)[0:B, BN:BN + NK])
                emptied(last, piece)

            def front(piece):
                kind = piece[0]
                if kind == "squares":
                    if piece[1] == 2:
                        dve.wait_ge(x2_loaded, 16 * BT)
                    if piece[1] == 7:
                        dve.wait_ge(pool_stored, 32)
                    squares(piece[1])
                if kind == "normed":
                    normed_rows(piece[1])
                if kind == "small":
                    conv_consts()
                if kind == "p" and piece[2] == "x":
                    conv_input(piece[1], piece[3])
                if kind == "p" and piece[2] == "b":
                    convolved(piece[1], piece[3])
                if kind == "attend":
                    attend(*piece[1:])
                if kind == "sample":
                    sample_attention()
                if kind == "wo":
                    projected(*piece[1:])
                if kind == "pl":
                    pool_added(*piece[1:])
                if piece == ("mixed", 0):
                    dve.wait_ge(rows_normed, rows_by(4))
                    V.tensor_copy(prev_rows, Hv[:, BT, :]).then_inc(prev_saved, 1)
                    dve.wait_ge(prev_saved, 1)
                if kind == "sc":
                    key_scores(*piece[1:])
                if kind == "scored":
                    for hc in range(HC):
                        wait_emptied(dve, ("sc", *piece[1:], hc))

            def search(part, src, st, offset):
                sums = cand.rearrange("p (a b) -> p a b", a=TOP)
                if part == 0:
                    step(V.tensor_copy(sc.rearrange("p c k -> p (c k)"), src))
                    step(V.max(sv[:, 0, 0:8], sc[:, 0, :]))
                if part == 1:
                    step(V.max_index(si[:, 0, 0:8], sv[:, 0, 0:8], sc[:, 0, :]))
                    step(V.match_replace(scw[:, 0, :], sv[:, 0, 0:8], sc[:, 0, :], LOWEST))
                if part == 2:
                    step(V.max(sv[:, 0, 8:16], scw[:, 0, :]))
                    step(V.max_index(si[:, 0, 8:16], sv[:, 0, 8:16], scw[:, 0, :]))
                if part == 3:
                    step(V.max(sv[:, 1, 0:8], sc[:, 1, :]))
                    step(V.max_index(si[:, 1, 0:8], sv[:, 1, 0:8], sc[:, 1, :]))
                if part == 4:
                    step(V.match_replace(scw[:, 1, :], sv[:, 1, 0:8], sc[:, 1, :], LOWEST))
                    step(V.max(sv[:, 1, 8:16], scw[:, 1, :]))
                if part == 5:
                    step(V.max_index(si[:, 1, 8:16], sv[:, 1, 8:16], scw[:, 1, :]))
                    step(V.tensor_tensor(sums, sv[:, 0, :].unsqueeze(2).to_broadcast([P, TOP, TOP]),
                                         sv[:, 1, :].unsqueeze(1).to_broadcast([P, TOP, TOP]), ALU.add))
                if part == 6:
                    step(V.max(cs[:, st, 0:8], cand))
                    step(V.max_index(ci[:, 0:8], cs[:, st, 0:8], cand))
                if part == 7:
                    step(V.match_replace(candw, cs[:, st, 0:8], cand, LOWEST))
                    step(V.max(cs[:, st, 8:16], candw))
                if part == 8:
                    V.tensor_scalar(ncs[:, st:st + 1], cs[:, st, 0:1], -1.0, None, ALU.mult).then_inc(cs_ready, 1)
                    step(V.max_index(ci[:, 8:16], cs[:, st, 8:16], candw))
                if part == 9:
                    step(V.tensor_scalar(cij[:, 0, :], ci[:], 4, None, ALU.logical_shift_right))
                    step(V.tensor_scalar(cij[:, 1, :], ci[:], TOP - 1, None, ALU.bitwise_and))
                    step(V.tensor_copy(cijf[:], cij[:]))
                if part == 10:
                    step(V.tensor_copy(sif[:], si[:]))
                    step(V.tensor_tensor(onehot[:], cijf[:].unsqueeze(3).to_broadcast([P, 2, TOP, TOP]),
                                         iota16[:].unsqueeze(1).unsqueeze(1).to_broadcast([P, 2, TOP, TOP]), ALU.is_equal))
                if part == 11:
                    step(V.tensor_tensor(onehot[:], onehot[:], sif[:].unsqueeze(2).to_broadcast([P, 2, TOP, TOP]), ALU.mult))
                if part == 12:
                    step(V.tensor_reduce(picked[:], onehot[:], AX.X, ALU.add))
                    step(V.tensor_scalar(picked[:, 0, :], picked[:, 0, :], float(NK), float(offset), ALU.mult, ALU.add))
                if part == 13:
                    V.tensor_tensor(idx[:, st, :], picked[:, 0, :], picked[:, 1, :], ALU.add).then_inc(idx_ready, 1)

            def product(st, tau, n, row, k):
                s = k % U_SLOTS
                dve.wait_ge(u_landed[s], tau * (16 * TOP // U_SLOTS) + 16 * (k // U_SLOTS + 1))
                V.tensor_tensor_reduce(out=u_rows[0:n, s, :], in0=u_rows[0:n, s, :], in1=row, scale=1.0, scalar=0.0,
                                       op0=ALU.mult, op1=ALU.add,
                                       accum_out=dots[0:n, st, k:k + 1]).then_inc(u_freed, 1)

            def weigh(par, tau, n):
                dve.wait_ge(gates_exp, tau + 1)
                step(V.reciprocal(rsum[0:n, :], exsum[0:n, par:par + 1]))
                dve.wait_ge(gelu_done, tau + 1)
                V.scalar_tensor_tensor(out=gate[0:n, par, :], in0=ex[0:n, par, :], scalar=rsum[0:n, :],
                                       in1=act_h[0:n, par, :], op0=ALU.mult, op1=ALU.mult).then_inc(gate_ready, 1)

            Xf = X[:, :, :].rearrange("p s d -> p (s d)")

            def add_unit(tasks, at, n=P):
                dve.wait_ge(v_freed, V_SLOTS + tasks * TOP)
                for half in range(2):
                    row = Xf[0:n, bass.ds(at + half * 512, 512)]
                    last = V.tensor_tensor(row, PSUM[0:n, 6 + half, :], row, ALU.add)
                last.then_inc(acc_added, 1)

            NT = 2 * NK

            def tile_unit(l, i, between):
                step(V.tensor_copy(hcur[:], H[:, bass.ds((i + 1) * D, D)]))
                for h in range(PH):
                    now = task(l, 0, h)
                    tau = i * PH + now
                    for k in range(TOP):
                        product(now % SETS, tau, P, hcur[:], k)
                        search(k, SC[:, bass.ds((i * PH + h + 1) * NT, NT)], (now + 1) % SETS, l * NE)
                        if between:
                            for piece in AGENDA.get((task(l, i, h) - 1) * TOP + k, ()):
                                front(piece)
                    if h == 0 and (not between or i):
                        add_unit(i * PH + task(l, 0, 0), i * D)
                    elif h == 0 and l:
                        add_unit(task(l, 0, 0), 0, B)
                    weigh(now % SETS, tau, P)

            dve.wait_ge(x_loaded, 16 * (BT + 1))
            for piece, _ in pieces(0, 0):
                front(piece)
            dve.wait_ge(own_stored, 48)
            dve.sem_inc(u_freed, U_SLOTS)
            for part in range(TOP):
                search(part, SC[:, 0:NT], 0, 0)
            for l in range(L):
                looped = 0 if l == 0 else BT
                for i in range(T - looped):
                    if i == T - 1:
                        sample_placed(0)
                    tile_unit(l, i, True)
                if looped:
                    sample_placed(1)
                    begin_loop()
                    with dve.Fori(T - looped, T) as i:
                        tile_unit(l, i, False)
                        end_body()
                    end_loop()
                tau = sample_task(l)
                dve.wait_ge(hrep_moved, 16 * PH * (l + 1))
                for k in range(TOP):
                    product(tau % SETS, tau, PH * B, hrep[0:PH * B, :], k)
                    if l == 0:
                        search(k, SC[:, 0:NT], (tau + 1) % SETS, NE)
                        for piece in AGENDA.get((tau - 1) * TOP + k, ()):
                            front(piece)
                add_unit(sample_task(l), T * D)
                weigh(tau % SETS, tau, PH * B)
            dve.wait_ge(acc_added, unit(1, T))
            squares(8)
            normed_rows(8)
            add_unit(L * TASKS, 0, B)
            dve.wait_ge(acc_added, unit(1, T + 1))
            squares(9)
            normed_rows(9)


_INS = ["x_prompt", "x_sample", "state_conv", "state_win_k", "state_win_v", "state_pool", "norm_mix", "w_in_ab",
        "conv_w", "w_out_ab", "pool_w", "pool_b", "pool_scale", "norm_ffn", "peer_wq", "peer_subkeys", "peer_u",
        "peer_v", "norm_final"]
_OUTS = [("y_prompt", (1, SEQ, D)), ("y_sample", (B, 1, D)), ("conv_prompt", (1, 1, 2, DA)),
         ("conv_sample", (1, B, 2, DA)), ("win_k_prompt", (1, SEQ, DA)), ("win_k_sample", (1, B, PAST, DA)),
         ("win_v_prompt", (1, SEQ, DA)), ("win_v_sample", (1, B, PAST, DA)),
         ("pool_prompt", (1, 1, PS, D)), ("pool_sample", (1, B, PS, D))]


def kernel(**inputs):
    import numpy as _np
    import concourse.bacc as _bacc
    from concourse.bass_utils import run_bass_kernel_spmd as _run

    nc = _bacc.Bacc("TRN2", target_bir_lowering=False, num_devices=1)
    arrays, args = {}, []
    for name in _INS:
        a = _np.ascontiguousarray(inputs[name])
        if name in ("state_win_k", "state_win_v"):
            a = a.reshape(1, B, PAST, DA)
        arrays[f"in_{name}"] = a
        args.append(nc.dram_tensor(f"in_{name}", a.shape, mybir.dt.from_np(a.dtype), kind="ExternalInput").ap())
    for name, shape in _OUTS:
        args.append(nc.dram_tensor(f"out_{name}", shape, f32, kind="ExternalOutput").ap())
    build(nc, *args)
    r = _run(nc, [arrays], core_ids=[0])
    out = {name: r.results[0][f"out_{name}"] for name, _ in _OUTS}
    for name in ("win_k_prompt", "win_v_prompt"):
        out[name] = out[name].reshape(1, 1, SEQ, NH, HD)
    for name in ("win_k_sample", "win_v_sample"):
        out[name] = out[name].reshape(1, B, PAST, NH, HD)
    return tuple(out[name] for name, _ in _OUTS)
```
